# Optimizing a Trainium2 kernel written in Bass

```python
import math
import jax, jax.numpy as jnp
from jax import lax
import numpy as np

D_MODEL = 1024
BATCH = 1
SEQ = 256
DEPTH = 4

GRID_W = 64
CTX_LEN = 256
N_MIXERS = 3
N_HEADS = 16
HEAD_DIM = D_MODEL // N_HEADS
WIN_H = 8
WIN_W = 16
CONV_W = 3
POOL_WINDOWS = (2, 4, 8, 16)
N_POOL_GROUPS = len(POOL_WINDOWS)
POOL_GC = D_MODEL // N_POOL_GROUPS
D_FF = ((8 * D_MODEL // 3 + 255) // 256) * 256
N_MOD = 6
EPS = 1e-6
N_LAYERS_A = (DEPTH + 2) // 3
N_LAYERS_B = (DEPTH + 1) // 3
N_LAYERS_C = DEPTH // 3

kernel_name = "hybrid_natten_shortconv_pool_dit"

def rms_norm(x, g):
    xf = x.astype(jnp.float32)
    y = xf * lax.rsqrt(jnp.mean(xf * xf, axis=-1, keepdims=True) + EPS)
    return (y * g.astype(jnp.float32)).astype(x.dtype)

def modulate(h, shift, scale):
    return h * (1 + scale) + shift

def swiglu(h, w1, w3, w2):
    return (jax.nn.silu(h @ w1) * (h @ w3)) @ w2

def neighbourhood_attention(hx, hc, w_qkv, w_o, rpb, need_ctx_out):
    B, N, D = hx.shape
    L = hc.shape[1]
    rows = N // GRID_W
    kh = min(WIN_H, rows)
    scale = HEAD_DIM ** -0.5

    qkv = (hx @ w_qkv).reshape(B, rows, GRID_W, 3, N_HEADS, HEAD_DIM)
    q = qkv[:, :, :, 0] * scale
    k = qkv[:, :, :, 1]
    v = qkv[:, :, :, 2]
    qkv_c = (hc @ w_qkv).reshape(B, L, 3, N_HEADS, HEAD_DIM)
    q_c = qkv_c[:, :, 0] * scale
    k_c = qkv_c[:, :, 1]
    v_c = qkv_c[:, :, 2]

    qc = np.arange(GRID_W)[:, None]
    kc = np.arange(GRID_W)[None, :]
    col_start = np.clip(qc - WIN_W // 2, 0, GRID_W - WIN_W)
    col_mask = (kc >= col_start) & (kc < col_start + WIN_W)
    dc_idx = np.clip(kc - qc, -(WIN_W - 1), WIN_W - 1) + (WIN_W - 1)
    rpb_cols = rpb.astype(jnp.float32)[:, :, dc_idx]

    def row_block(r):
        start = jnp.clip(r - kh // 2, 0, rows - kh)
        k_band = lax.dynamic_slice_in_dim(k, start, kh, axis=1)
        v_band = lax.dynamic_slice_in_dim(v, start, kh, axis=1)
        q_r = lax.dynamic_index_in_dim(q, r, axis=1, keepdims=False)
        dr_idx = start + jnp.arange(kh) - r + (WIN_H - 1)
        bias = jnp.take(rpb_cols, dr_idx, axis=1).transpose(0, 2, 1, 3)
        s_lat = jnp.einsum('bqhd,brkhd->bhqrk', q_r, k_band).astype(jnp.float32) + bias[None]
        s_lat = jnp.where(col_mask[None, None, :, None, :], s_lat, -jnp.inf)
        s_lat = s_lat.reshape(B, N_HEADS, GRID_W, kh * GRID_W)
        s_ctx = jnp.einsum('bqhd,blhd->bhql', q_r, k_c).astype(jnp.float32)
        p = jax.nn.softmax(jnp.concatenate([s_lat, s_ctx], axis=-1), axis=-1).astype(v.dtype)
        o = jnp.einsum('bhqk,bkhd->bqhd', p[..., :kh * GRID_W],
                       v_band.reshape(B, kh * GRID_W, N_HEADS, HEAD_DIM))
        o = o + jnp.einsum('bhql,blhd->bqhd', p[..., kh * GRID_W:], v_c)
        return o

    o = lax.map(row_block, jnp.arange(rows))
    yx = o.transpose(1, 0, 2, 3, 4).reshape(B, N, D) @ w_o

    yc = None
    if need_ctx_out:
        s = jnp.einsum('blhd,bmhd->bhlm', q_c, k_c).astype(jnp.float32)
        p = jax.nn.softmax(s, axis=-1).astype(v_c.dtype)
        yc = jnp.einsum('bhlm,bmhd->blhd', p, v_c).reshape(B, L, D) @ w_o
    return yx, yc

def dwconv3_centred(u, w):
    up = jnp.pad(u, ((0, 0), (1, 1), (0, 0)))
    return up[:, :-2] * w[0] + up[:, 1:-1] * w[1] + up[:, 2:] * w[2]

def short_conv_mixer(h, w_in, conv_w, w_out):
    gb, gc, val = jnp.split(h @ w_in, 3, axis=-1)
    return (gb * dwconv3_centred(gc * val, conv_w)) @ w_out

def multiscale_pool_mixer(h, w_grp, ch_scale):
    B, N, D = h.shape
    hf = h.astype(jnp.float32)
    cs = jnp.concatenate([jnp.zeros((B, 1, D), jnp.float32), jnp.cumsum(hf, axis=1)], axis=1)
    t = np.arange(N)
    outs = []
    for g, win in enumerate(POOL_WINDOWS):
        lo = np.maximum(t - win // 2, 0)
        hi = np.minimum(t + win // 2, N)
        cnt = (hi - lo).astype(np.float32)
        sl = slice(g * POOL_GC, (g + 1) * POOL_GC)
        mean = (cs[:, hi, sl] - cs[:, lo, sl]) / cnt[None, :, None]
        outs.append(mean - hf[..., sl])
    pooled = jnp.stack(outs, axis=2).astype(h.dtype)
    y = jnp.einsum('bngc,gcd->bngd', pooled, w_grp).reshape(B, N, D)
    return y * ch_scale

def setup_inputs(seed: int = 0) -> dict:
    key = jax.random.key(seed)
    ks = jax.random.split(key, 20)
    D, F = D_MODEL, D_FF
    f32 = jnp.float32

    def nrm(k, shape, s):
        return jax.random.normal(k, shape, f32) * s

    return {
        "x": nrm(ks[0], (BATCH, SEQ, D), 1.0),
        "c": nrm(ks[1], (BATCH, D), 1.0),
        "ctx": nrm(ks[2], (BATCH, CTX_LEN, D), 1.0),
        "c_ctx": nrm(ks[3], (D,), 1.0),
        "adaln_w": nrm(ks[4], (DEPTH, D, N_MOD * D), 0.5 * D ** -0.5),
        "adaln_b": nrm(ks[5], (DEPTH, N_MOD * D), 0.02),
        "norm_mix_g": 1.0 + nrm(ks[6], (DEPTH, D), 0.05),
        "norm_ffn_g": 1.0 + nrm(ks[7], (DEPTH, D), 0.05),
        "ffn_w1": nrm(ks[8], (DEPTH, D, F), D ** -0.5),
        "ffn_w3": nrm(ks[9], (DEPTH, D, F), D ** -0.5),
        "ffn_w2": nrm(ks[10], (DEPTH, F, D), F ** -0.5),
        "na_w_qkv": nrm(ks[11], (N_LAYERS_A, D, 3 * D), D ** -0.5),
        "na_w_o": nrm(ks[12], (N_LAYERS_A, D, D), D ** -0.5),
        "na_rpb": nrm(ks[13], (N_LAYERS_A, N_HEADS, 2 * WIN_H - 1, 2 * WIN_W - 1), 0.2),
        "sc_w_in": nrm(ks[14], (N_LAYERS_B, D, 3 * D), D ** -0.5),
        "sc_conv_w": nrm(ks[15], (N_LAYERS_B, CONV_W, D), CONV_W ** -0.5),
        "sc_w_out": nrm(ks[16], (N_LAYERS_B, D, D), D ** -0.5),
        "pool_w": nrm(ks[17], (N_LAYERS_C, N_POOL_GROUPS, POOL_GC, POOL_GC), POOL_GC ** -0.5),
        "pool_scale": 1.0 + nrm(ks[18], (N_LAYERS_C, D), 0.1),
        "final_g": 1.0 + nrm(ks[19], (D,), 0.05),
    }

def reference(x, c, ctx, c_ctx, adaln_w, adaln_b, norm_mix_g, norm_ffn_g, ffn_w1, ffn_w3, ffn_w2,
              na_w_qkv, na_w_o, na_rpb, sc_w_in, sc_conv_w, sc_w_out, pool_w, pool_scale, final_g):
    silu_c = jax.nn.silu(c)
    silu_cc = jax.nn.silu(c_ctx)
    for layer in range(DEPTH):
        kind = layer % N_MIXERS
        j = layer // N_MIXERS
        need_ctx_out = layer < DEPTH - 1

        mx = jnp.split((silu_c @ adaln_w[layer] + adaln_b[layer])[:, None, :], N_MOD, axis=-1)
        mc = jnp.split(silu_cc @ adaln_w[layer] + adaln_b[layer], N_MOD, axis=-1)

        hx = modulate(rms_norm(x, norm_mix_g[layer]), mx[0], mx[1])
        if kind == 0 or need_ctx_out:
            hc = modulate(rms_norm(ctx, norm_mix_g[layer]), mc[0], mc[1])

        if kind == 0:
            yx, yc = neighbourhood_attention(hx, hc, na_w_qkv[j], na_w_o[j], na_rpb[j], need_ctx_out)
        elif kind == 1:
            yx = short_conv_mixer(hx, sc_w_in[j], sc_conv_w[j], sc_w_out[j])
            yc = short_conv_mixer(hc, sc_w_in[j], sc_conv_w[j], sc_w_out[j]) if need_ctx_out else None
        else:
            yx = multiscale_pool_mixer(hx, pool_w[j], pool_scale[j])
            yc = multiscale_pool_mixer(hc, pool_w[j], pool_scale[j]) if need_ctx_out else None

        x = x + mx[2] * yx
        hx = modulate(rms_norm(x, norm_ffn_g[layer]), mx[3], mx[4])
        x = x + mx[5] * swiglu(hx, ffn_w1[layer], ffn_w3[layer], ffn_w2[layer])

        if need_ctx_out:
            ctx = ctx + mc[2] * yc
            hc = modulate(rms_norm(ctx, norm_ffn_g[layer]), mc[3], mc[4])
            ctx = ctx + mc[5] * swiglu(hc, ffn_w1[layer], ffn_w3[layer], ffn_w2[layer])
    return rms_norm(x, final_g)


_drawn_inputs = setup_inputs


def setup_inputs(seed=0):
    import zlib

    import numpy as np

    out = dict(_drawn_inputs(seed))
    spreads = {}
    factors = {'na_rpb': 8.0}
    for name, (base, spread) in spreads.items():
        noise = np.random.default_rng([zlib.crc32(name.encode()), seed]).standard_normal(out[name].shape)
        drawn = base * np.exp(spread * noise) if base else spread * noise
        out[name] = __import__('jax').numpy.asarray(drawn.astype(out[name].dtype))
    for name, factor in factors.items():
        out[name] = (out[name] * factor).astype(out[name].dtype)
    return out
```

```python
from contextlib import ExitStack
from typing import NamedTuple

import numpy as np

import concourse.bass as bass
from concourse import mybir

F32 = mybir.dt.float32
F32R = mybir.dt.float32r
ALU = mybir.AluOpType
ACT = mybir.ActivationFunctionType
AXX = mybir.AxisListType.X

P = 128
EPS = 1e-6
GRID_W = 64
WIN_W = 16
CONV_W = 3
POOL_WINDOWS = (2, 4, 8, 16)
N_MOD = 6
BIG = 3.0e38
UC = 256
AC = 512
PAD = 8


class Phase(NamedTuple):
    name: str
    layer: int
    units: int
    slabs: int
    tokens: int
    unit0: int
    fresh: bool = False
    ada_iters: int = 0
    ada_layer: int = 0
    ada_group: int = 0
    ada_unit0: int = 0
    chunk0: int = 0
    tile0: int = 0


def sections(ph):
    total = ph.units // 2
    cuts = sorted({0, min(ph.ada_iters, total), total - 1, total})
    for a, b in zip(cuts, cuts[1:]):
        yield a, b - a, a < ph.ada_iters, a == total - 1


def iterate(eng, first, count, body):
    if count == 1:
        body(first)
    else:
        with eng.Fori(first, first + count) as i:
            body(i)


def plan(kt, ff_tiles, depth, n_tok, n_lat):
    phases = []
    counts = {"unit": 0, "ada": 0, "chunk": 0}
    groups = N_MOD * kt * P // AC

    def add(name, layer, units, slabs, tokens, ada_iters=0, ada_layer=0, ada_group=0, chunks=0, **kw):
        phases.append(Phase(name, layer, units, slabs, tokens, counts["unit"], ada_iters=ada_iters,
                            ada_layer=ada_layer, ada_group=ada_group, ada_unit0=counts["ada"],
                            chunk0=counts["chunk"], **kw))
        counts["unit"] += units
        counts["ada"] += 2 * ada_iters
        counts["chunk"] += chunks

    wide = kt * P // UC
    half = (ff_tiles // 2 + 1) // 2 * 2
    for layer in range(depth):
        kind = layer % 3
        last = layer == depth - 1
        tok = n_lat if last else n_tok
        own = 2 if layer == 0 else 0
        if kind == 0:
            add("q", layer, wide, kt, tok, fresh=True, ada_iters=own, ada_group=4)
            add("k", layer, wide, kt, n_tok, ada_iters=own, ada_group=6)
            add("v", layer, wide, kt, n_tok, ada_iters=own, ada_group=8)
            add("wo", layer, wide, kt, tok, ada_iters=own, ada_group=10)
        elif kind == 1:
            add("conv", layer, 2 * wide, kt, tok, fresh=True)
            add("gateb", layer, wide, kt, tok, chunks=wide)
            add("scout", layer, wide, kt, tok)
        else:
            add("pool", layer, len(POOL_WINDOWS), kt // len(POOL_WINDOWS), tok, chunks=wide)
        nxt = 0 if last else 1
        tiles = (half, ff_tiles - half)
        per = [nxt * tiles[0] // 2, nxt * 2]
        per.append(nxt * (groups - sum(per)))
        add("up", layer, tiles[0], kt, tok, per[0], layer + 1, 0, tiles[0] // 2, fresh=True)
        add("down", layer, 2 * wide, tiles[0] // 2, tok, per[1], layer + 1, per[0])
        add("up", layer, tiles[1], kt, tok, per[2], layer + 1, per[0] + per[1], tiles[1] // 2,
            tile0=tiles[0])
        add("down", layer, 2 * wide, tiles[1] // 2, tok, tile0=tiles[0])
    return phases


def build(nc, x, c, ctx, c_ctx, adaln_w, adaln_b, norm_mix_g, norm_ffn_g, ffn_w1, ffn_w3, ffn_w2,
          na_w_qkv, na_w_o, na_rpb, sc_w_in, sc_conv_w, sc_w_out, pool_w, pool_scale, final_g, out):
    _, SEQ, D = x.shape
    CTX = ctx.shape[1]
    DEPTH = adaln_w.shape[0]
    FF = ffn_w1.shape[2]
    HEADS, DR, DC = na_rpb.shape[1:]
    KT = D // P
    TOK = SEQ + CTX
    ROWS = SEQ // GRID_W
    HD = D // HEADS
    SCALE = float(HD) ** -0.5
    FT = FF // P
    NC = N_MOD * KT
    AG = AC // P
    assert (SEQ, CTX, HD, DEPTH, DR // 2 + 1) == (256, 256, 64, 4, 8) and ROWS <= 8 and FF % UC == 0

    phases = plan(KT, FT, DEPTH, TOK, SEQ)
    following = dict(zip(range(len(phases)), phases[1:]))
    HALF = phases[[p.name for p in phases].index("up")].units

    place = [(nc.sbuf_base + 63) // 64 * 64]

    def at(name, shape, dt, offset):
        return nc.alloc_sbuf_tensor_at(name, [P] + shape, dt, offset=offset)

    def new(name, shape, dt=F32):
        t = at(name, shape, dt, place[0])
        place[0] += (int(np.prod(shape)) * 4 + 63) // 64 * 64
        return t

    xT = new("xT", [KT, TOK])
    hhi = new("hhi", [KT, TOK], F32R)
    hlo_at = place[0]
    hlo = new("hlo", [KT, TOK], F32R)
    raw = new("raw", [2, 8, UC])
    whi = new("whi", [2, 8, UC], F32R)
    wlo = new("wlo", [2, 8, UC], F32R)
    araw_at = place[0]
    araw = new("araw", [2, 4, AC])
    acc = new("acc", [2, AC])
    u_at = place[0]
    uhi = new("uhi", [HALF, TOK], F32R)
    ulo = new("ulo", [HALF, TOK], F32R)
    qT = at("qT", [KT, TOK], F32, u_at)
    kT = at("kT", [KT, TOK], F32, u_at + KT * TOK * 4)
    vt = at("vt", [TOK // P, D], F32, u_at + 2 * KT * TOK * 4)
    yhi = at("yhi", [KT, TOK], F32R, u_at)
    ylo = at("ylo", [KT, TOK], F32R, u_at + KT * TOK * 4)
    cv = at("cv", [KT, TOK], F32, u_at + 2 * KT * TOK * 4)
    PW = SEQ + 2 * PAD
    hp = at("hp", [KT * 2, PW], F32, u_at)
    pw = at("pw", [3, 2, 4, PW], F32, u_at + KT * 2 * PW * 4)
    fin = at("fin", [KT, SEQ], F32, u_at)
    fout = at("fout", [SEQ // P, D], F32, u_at + KT * SEQ * 4)
    PG = 2 * D // AC
    apro = [at(f"apro{g}", [KT, AC], F32, u_at + g * KT * AC * 4) for g in range(PG - 1)]
    apro += [at(f"apro{PG - 1}", [KT, AC], F32, araw_at)]
    xtok = at("xtok", [TOK // P, D], F32, hlo_at)
    work_at = place[0]
    TR = 3
    gs = new("gs", [2, TOK])
    tb = new("tb", [2, TOK])
    sq = new("sq", [2, TOK])
    acc2 = new("acc2", [2, TOK])
    rstd = new("rstd", [TOK])
    tr = new("tr", [TR, TOK])
    prob = at("prob", [4, TOK], F32, work_at)
    ptsb = at("ptsb", [2, TOK], F32, work_at + 4 * TOK * 4)
    otok = at("otok", [TOK // P, P], F32, work_at + 6 * TOK * 4)
    stage = at("stage", [3, P], F32, work_at)
    arow = at("arow", [2, AC], F32, work_at + 2 * TOK * 4)
    braw = new("braw", [2, 2, ROWS * GRID_W])
    biasm = new("biasm", [2, 2, ROWS * GRID_W])
    ones = new("ones", [P])
    ident = new("ident", [P])
    flip = new("flip", [P])
    mask = new("mask", [GRID_W])
    ratio = new("ratio", [len(POOL_WINDOWS), 2 * PAD])
    vecs = new("vecs", [3 * P])
    sc = new("sc", [KT, 2])
    modv = new("modv", [2, 2, NC])
    moda = new("moda", [2, KT])
    pgate = new("pgate", [2, KT])
    epst = new("epst", [1])
    nmx = new("nmx", [8])
    mx = new("mx", [2, 8])
    rsum = new("rsum", [8])
    rinv = new("rinv", [8])
    assert place[0] <= nc.sbuf_usable_end, place[0]

    pair = [nc.alloc_psum_tensor(f"pair{p}", [P, 2, 512], F32) for p in range(2)]
    sbank = [pair[0][:, 0, :], pair[0][:, 1, :], pair[1][:, 0, :], pair[1][:, 1, :]]
    ptb = [nc.alloc_psum_tensor(f"ptb{p}", [P, 512], F32) for p in range(2)]
    adap = nc.alloc_psum_tensor("adap", [P, 512], F32)
    ssp = nc.alloc_psum_tensor("ssp", [P, 512], F32)
    obank = [adap, ssp]
    psP = [pair[p][:, :, :] for p in range(2)]

    V_B = 0
    V_GM = DEPTH * NC
    V_GF = V_GM + DEPTH * KT
    V_CW = V_GF + DEPTH * KT
    V_PS = V_CW + CONV_W * KT
    V_FG = V_PS + KT
    V_C = V_FG + KT
    V_END = V_C + 2 * KT
    small = [
        (adaln_b.rearrange("l (n p) -> (l n) p", p=P), V_B),
        (norm_mix_g.rearrange("l (n p) -> (l n) p", p=P), V_GM),
        (norm_ffn_g.rearrange("l (n p) -> (l n) p", p=P), V_GF),
        (sc_conv_w[0].rearrange("l (n p) -> (l n) p", p=P), V_CW),
        (pool_scale.rearrange("l (n p) -> (l n) p", p=P), V_PS),
        (final_g.rearrange("(n p) -> n p", p=P), V_FG),
        (c.rearrange("l (n p) -> (l n) p", p=P), V_C),
        (c_ctx.rearrange("(n p) -> n p", p=P), V_C + KT),
    ]
    small_parts = []
    for src, col in small:
        r = 0
        while r < src.shape[0]:
            n = min(src.shape[0] - r, P - (col + r) % P)
            small_parts.append((src[r:r + n, :], (col + r) // P, (col + r) % P, n))
            r += n

    def sem(name):
        return nc.alloc_semaphore(name)

    raw_in = [sem("raw_in0"), sem("raw_in1")]
    ada_in = [sem("ada_in0"), sem("ada_in1")]
    hi_done, lo_done, pe_done = sem("hi_done"), sem("lo_done"), sem("pe_done")
    drained = [sem("drained0"), sem("drained1")]
    ada_ops, ada_reduced = sem("ada_ops"), sem("ada_reduced")
    gs_ready, tb_ready, uhi_done, u_done = sem("gs_ready"), sem("tb_ready"), sem("uhi_done"), sem("u_done")
    conv_ops = sem("conv_ops")
    xt_done, sq_done, acc_done, ss_done, sd_done = (sem("xt_done"), sem("sq_done"), sem("acc_done"),
                                                     sem("ss_done"), sem("sd_done"))
    t_done, hh_done, h_done = sem("t_done"), sem("hh_done"), sem("h_done")
    chain_s = sem("dve_chain")
    s_done, mx_done, nm_done, p_done = sem("s_done"), sem("mx_done"), sem("nm_done"), sem("p_done")
    tr_done, pt_done, pv_done, ri_done, o_done = (sem("tr_done"), sem("pt_done"), sem("pv_done"),
                                                  sem("ri_done"), sem("o_done"))
    ot_done, ot_hi, ot_free = sem("ot_done"), sem("ot_hi"), sem("ot_free")
    bias_in = [sem("bias_in0"), sem("bias_in1")]
    bias_ready = sem("bias_ready")
    small_in, x_in = sem("small_in"), [sem("x_in0"), sem("x_in1")]
    apro_in = [sem(f"apro_in{g}") for g in range(PG)]
    arow_done, arow_out = sem("arow_done"), sem("arow_out")
    pool_c, consts = sem("pool_chain"), sem("consts")
    vt_done, vecs_done, silu_done, apro_done = sem("vt_done"), sem("vecs_done"), sem("silu_done"), sem("apro_done")
    xtr_done, x_init = sem("xtr_done"), sem("x_init")
    pads_ready, sums_ready = sem("pads_ready"), sem("sums_ready")
    fin_tr, fin_ev, stored = sem("fin_tr"), sem("fin_ev"), sem("stored")

    def norm_tokens(r):
        return SEQ if r >= 2 * DEPTH - 1 else TOK

    ATT = [layer for layer in range(DEPTH) if layer % 3 == 0]
    JOBS = {layer: (2 * SEQ // P if layer == DEPTH - 1 else 2 * TOK // P) for layer in ATT}
    JBASE = {layer: sum(KT * JOBS[m] for m in ATT if m < layer) for layer in ATT}

    def job(layer, idx):
        per = JOBS[layer] // 2
        return idx // per, idx % per

    def width(qt):
        return TOK if qt < SEQ // P else CTX

    def finals(ph):
        return ph.name in ("wo", "scout", "pool") or (ph.name == "down" and ph.tile0 > 0)

    def norm_of(ph):
        return 2 * ph.layer + (2 if ph.name == "down" else 1)

    def pair_base(r):
        return (KT // 2) * (r - 1)

    def h_base(r):
        return KT * sum(1 for q in range(r) if not pools(q))

    def pools(r):
        return r % 2 == 0 and (r // 2) % 3 == 2 and r < 2 * DEPTH

    def cols(s):
        return slice(s * SEQ, (s + 1) * SEQ)

    def ada_src(layer, group, half):
        v = adaln_w[layer].rearrange("(k p) n -> p k n", p=P)
        return v[:, 4 * half:4 * half + 4, bass.ds(group * AC, AC)]

    def weight_src(ph, i, par):
        att = ph.layer // 3
        u = i * 2 + par
        rows = "(k p) n -> p k n"
        if ph.name in "qkv":
            return na_w_qkv[att].rearrange(rows, p=P)[:, :, bass.ds(u * UC + "qkv".index(ph.name) * D, UC)]
        if ph.name == "wo":
            return na_w_o[att].rearrange(rows, p=P)[:, :, bass.ds(u * UC, UC)]
        if ph.name == "conv":
            return sc_w_in[0].rearrange(rows, p=P)[:, :, bass.ds(i * UC + (1 + par) * D, UC)]
        if ph.name == "gateb":
            return sc_w_in[0].rearrange(rows, p=P)[:, :, bass.ds(u * UC, UC)]
        if ph.name == "scout":
            return sc_w_out[0].rearrange(rows, p=P)[:, :, bass.ds(u * UC, UC)]
        if ph.name == "pool":
            return pool_w[0, u].rearrange(rows, p=P)
        if ph.name == "up":
            w = (ffn_w1, ffn_w3)[par][ph.layer]
            return w.rearrange(rows, p=P)[:, :, bass.ds(i * UC + ph.tile0 * P, UC)]
        k0 = ph.tile0 + par * ph.slabs
        return ffn_w2[ph.layer].rearrange(rows, p=P)[:, k0:k0 + ph.slabs, bass.ds(i * UC, UC)]

    def window_sums(g, eng, link):
        src, lo, hi, step, k = hp[:, 4 * g:4 * g + 4, :], 0, PW, 1, 0
        ins = None
        while 2 * step <= POOL_WINDOWS[g]:
            if ins:
                link(ins)
            dst = pw[:, 2 if g == len(POOL_WINDOWS) - 1 else g % 2, k % 2, :, :]
            back, fwd = (1, 0) if step == 1 else (step // 2, step // 2)
            lo, hi = lo + back, hi - fwd
            ins = eng.tensor_tensor(dst[:, :, lo:hi], src[:, :, lo - back:hi - back],
                                    src[:, :, lo + fwd:hi + fwd], ALU.add)
            src, step, k = dst, 2 * step, k + 1
        return ins

    with nc.Block() as block:
        @block.sync
        def _(sp):
            def load(ph, i, par):
                n = i * 2 + (ph.unit0 + par)
                if not (isinstance(i, int) and n < 2):
                    sp.wait_ge(lo_done, n - 1)
                sp.dma_start(raw[:, par, 0:ph.slabs, :], weight_src(ph, i, par)).then_inc(raw_in[par], 16)

            def load_ada(ph, i, par):
                a = i * 2 + (ph.ada_unit0 + par)
                if not (isinstance(i, int) and a < 2):
                    sp.wait_ge(ada_ops, a * 8 - 8)
                elif a < 2:
                    sp.wait_ge(apro_done, PG)
                sp.dma_start(araw[:, par, :, :], ada_src(ph.ada_layer, i + ph.ada_group, par))\
                    .then_inc(ada_in[par], 16)

            x_v = x[0].rearrange("(t p) d -> p t d", p=P)
            ctx_v = ctx[0].rearrange("(t p) d -> p t d", p=P)
            ts = SEQ // P
            sp.dma_start(xtok[:, 0:ts, :], x_v).then_inc(x_in[0], 16)
            sp.dma_start(xtok[:, ts:TOK // P, :], ctx_v).then_inc(x_in[1], 16)
            sp.wait_ge(small_in, 16 * len(small_parts))
            for g in range(PG):
                src = adaln_w[0].rearrange("(k p) n -> p k n", p=P)[:, :, g * AC:(g + 1) * AC]
                sp.dma_start(apro[g][:, :, :], src).then_inc(apro_in[g], 16)
            load(phases[0], 0, 0)
            load(phases[0], 0, 1)

            def biases(layer):
                a = ATT.index(layer)
                for h in range(HEADS):
                    if a or h >= 2:
                        sp.wait_ge(bias_ready, a * HEADS + h - 1)
                    for rq in range(ROWS):
                        r0 = rq % 2 * GRID_W
                        off = (a * HEADS + h) * DR * DC + (DR // 2 - rq) * DC + DC // 2 - (GRID_W - 1)
                        src = bass.AP(na_rpb.tensor, off, [[1, GRID_W], [DC, ROWS], [1, GRID_W]])
                        dst = braw[r0:r0 + GRID_W, h % 2, rq // 2, :].rearrange("p (r c) -> p r c", r=ROWS)
                        sp.dma_start(dst, src).then_inc(bias_in[h % 2], 16)

            for k, ph in enumerate(phases):
                nxt = following.get(k)
                for first, count, ada, last in sections(ph):
                    def body(i):
                        for par in range(2):
                            if not last:
                                load(ph, i + 1, par)
                            elif nxt:
                                load(nxt, 0, par)
                            if ada:
                                load_ada(ph, i, par)
                    iterate(sp, first, count, body)
                if ph.name == "v":
                    biases(ph.layer)
            for t in range(SEQ // P):
                sp.wait_ge(fin_ev, 2 * (t + 1))
                sp.dma_start(out[0, t * P:(t + 1) * P, :], fout[:, t, :]).then_inc(stored, 16)
            sp.wait_ge(stored, 16 * (SEQ // P))

        @block.gpsimd
        def _(pool):
            links = [0]

            def link(ins):
                links[0] += 1
                ins.then_inc(pool_c, 1)
                pool.wait_ge(pool_c, links[0])

            link(nc.gpsimd.memset(ident[:, :], 0.0))
            nc.gpsimd.affine_select(out=ident[:, :], in_=ident[:, :], compare_op=ALU.not_equal, fill=1.0,
                                    base=0, pattern=[[-1, P]], channel_multiplier=1).then_inc(consts, 1)
            nc.gpsimd.memset(ones[:, :], 1.0).then_inc(consts, 1)
            nc.gpsimd.memset(epst[:, :], EPS).then_inc(consts, 1)
            pool.wait_ge(consts, 3)
            link(nc.gpsimd.memset(flip[:, :], 0.0))
            for p0 in range(0, P, GRID_W):
                m = flip[p0:p0 + GRID_W, :]
                ins = nc.gpsimd.affine_select(out=m, in_=m, compare_op=ALU.not_equal, fill=1.0,
                                              base=-(p0 + GRID_W - 1), pattern=[[1, P]], channel_multiplier=1)
                ins.then_inc(consts, 1)
                pool.wait_ge(consts, 4 + p0 // GRID_W)
            link(nc.gpsimd.memset(mask[:, :], 0.0))
            hw = WIN_W // 2
            for p0 in range(0, P, GRID_W):
                m = mask[p0:p0 + GRID_W, 0:GRID_W - WIN_W]
                link(nc.gpsimd.affine_select(out=m, in_=m, compare_op=ALU.is_ge, fill=-BIG,
                                             base=hw - (GRID_W - 1), pattern=[[1, GRID_W - WIN_W]],
                                             channel_multiplier=1))
                m = mask[p0:p0 + GRID_W, WIN_W:GRID_W]
                link(nc.gpsimd.affine_select(out=m, in_=m, compare_op=ALU.is_ge, fill=-BIG,
                                             base=GRID_W - 1 + hw - 1 - WIN_W,
                                             pattern=[[-1, GRID_W - WIN_W]], channel_multiplier=-1))
            for g, win in enumerate(POOL_WINDOWS):
                hw = win // 2
                for e in range(hw):
                    nc.gpsimd.memset(ratio[:, g, e:e + 1], win / (e + hw))
                for e in range(1, hw):
                    nc.gpsimd.memset(ratio[:, g, 2 * PAD - e:2 * PAD - e + 1], win / (e + hw))
            wide_mask = mask[:, :].unsqueeze(1).to_broadcast([P, 2 * ROWS, GRID_W])

            def widest_sums():
                r = [q for q in range(2 * DEPTH) if pools(q)][0]
                pool.wait_ge(hh_done, KT * (r + 1))
                pool.wait_ge(pads_ready, 1)
                window_sums(len(POOL_WINDOWS) - 1, nc.gpsimd, link).then_inc(sums_ready, 1)

            for a, layer in enumerate(ATT):
                J, B = JOBS[layer], JBASE[layer]

                def masks(j, start):
                    for par in range(2):
                        pool.wait_ge(bias_in[par], (j + (a * KT + 1)) * 16 * ROWS)
                        if not start:
                            pool.wait_ge(nm_done, j * J + (B - J + par * (J // 2) + 2))
                        elif a:
                            pool.wait_ge(nm_done, B)
                        nc.gpsimd.tensor_tensor(
                            biasm[:, par, :, :].rearrange("p q (r c) -> p (q r) c", c=GRID_W),
                            braw[:, par, :, :].rearrange("p q (r c) -> p (q r) c", c=GRID_W),
                            wide_mask, ALU.add).then_inc(bias_ready, 1)
                masks(0, True)
                with pool.Fori(1, KT) as j:
                    masks(j, False)
                if a == 0:
                    widest_sums()

        @block.tensor
        def _(pe):
            mm, tp = nc.tensor.matmul, nc.tensor.transpose

            def reduce_ada(ph, i):
                a = i * 2 + (ph.ada_unit0 + 1)
                pe.wait_ge(ada_ops, a * 8 + 8)
                for s in range(2):
                    for t in range(AG):
                        col = (i + ph.ada_group) * AG + (s * NC + t)
                        ins = mm(adap[:, bass.ds(col, 1)], acc[:, s, t * P:(t + 1) * P], ones[:, 0:1],
                                 start=True, stop=True)
                ins.then_inc(ada_reduced, 1)

            def source(ph, kt, par):
                n = slice(0, ph.tokens)
                if ph.name == "down":
                    t = par * ph.slabs + kt
                    return uhi[:, t, n], ulo[:, t, n]
                if ph.name == "scout":
                    return yhi[:, kt, n], ylo[:, kt, n]
                return hhi[:, kt, n], hlo[:, kt, n]

            def slab_wait(ph, i, par, kt):
                if ph.fresh and par == 0:
                    r = 2 * ph.layer + (1 if ph.name == "up" else 0)
                    pe.wait_ge(h_done, h_base(r) + kt + 1)
                elif ph.name == "scout" and par == 0 and kt % 2 == 0:
                    pe.wait_ge(u_done, ph.chunk0 - KT // 2 + kt // 2 + 1)
                elif ph.name == "down" and (par * ph.slabs + kt) % 2 == 0 or ph.name == "down" and kt == 0:
                    chunks = (HALF if ph.tile0 == 0 else FT - HALF) // 2
                    pe.wait_ge(u_done, ph.chunk0 - chunks + (par * ph.slabs + kt) // 2 + 1)

            def unit(ph, i, par, start, reduced=None):
                n = i * 2 + (ph.unit0 + par)
                if ph.name == "pool":
                    pe.wait_ge(u_done, ph.chunk0 + 2 * i + par + 1)
                pe.wait_ge(lo_done, n + 1)
                if not (isinstance(i, int) and n < 2):
                    pe.wait_ge(drained[par], i + ph.unit0 // 2)
                out = pair[par]
                if ph.name == "v":
                    for tt in range(ph.tokens // P):
                        t = slice(tt * P, (tt + 1) * P)
                        o = out[:, tt // 2, tt % 2 * UC:(tt % 2 + 1) * UC]
                        for kt in range(ph.slabs):
                            mm(o, hhi[:, kt, t], whi[:, par, kt, :], start=kt == 0, stop=False)
                            mm(o, hlo[:, kt, t], whi[:, par, kt, :], start=False, stop=False)
                            ins = mm(o, hhi[:, kt, t], wlo[:, par, kt, :], start=False,
                                     stop=kt == ph.slabs - 1)
                        if reduced and tt == 0:
                            reduce_ada(*reduced)
                    ins.then_inc(pe_done, 1)
                    return
                for kt in range(ph.slabs):
                    if start:
                        slab_wait(ph, i, par, kt)
                    k0 = 2 * (2 * i + par) if ph.name == "pool" else 0
                    a, b = source(ph, k0 + kt, par)
                    for m in range(2):
                        w = slice(m * P, (m + 1) * P)
                        o = out[:, m, 0:ph.tokens]
                        mm(o, whi[:, par, kt, w], a, start=kt == 0, stop=False)
                        mm(o, whi[:, par, kt, w], b, start=False, stop=False)
                        ins = mm(o, wlo[:, par, kt, w], a, start=False, stop=kt == ph.slabs - 1)
                    if reduced and kt == 1:
                        reduce_ada(*reduced)
                ins.then_inc(pe_done, 1)

            def keep_warm(count):
                for _ in range(count):
                    mm(ptb[1][:, 0:P], ident[:, :], ident[:, :], start=True, stop=True)

            def sum_squares(r):
                n = norm_tokens(r)
                pe.wait_ge(acc_done, 7 * (r + 1))
                mm(ssp[:, 0:n], ones[:, :], acc2[:, 0, 0:n], start=True, stop=False)
                mm(ssp[:, 0:n], ones[:, :], acc2[:, 1, 0:n], start=False, stop=False)
                for m in range(2):
                    pe.wait_ge(sq_done, KT * r + KT - 1 + m)
                    ins = mm(ssp[:, 0:n], ones[:, :], sq[:, m, 0:n], start=False, stop=m == 1)
                ins.then_inc(ss_done, 1)

            def attention(layer):
                J, B = JOBS[layer], JBASE[layer]
                NJ = J * KT
                last_v = [p for p in phases if p.name == "v" and p.layer == layer][0]
                uses = (last_v.unit0 + last_v.units) // 2
                keep_warm(6)
                pe.wait_ge(drained[0], uses)
                pe.wait_ge(drained[1], uses)

                def scores(t):
                    p, qt = job(layer, t % J)
                    j, f = t // J, slice(HD * p, HD * (p + 1))
                    w = width(qt)
                    if t >= 4:
                        pe.wait_ge(p_done, B + t - 3)
                    mm(sbank[t % 4][:, TOK - w:TOK], qT[f, j, qt * P:(qt + 1) * P], kT[f, j, TOK - w:TOK],
                       start=True, stop=True).then_inc(s_done, 1)

                def turn(t):
                    _, qt = job(layer, t % J)
                    pe.wait_ge(p_done, B + t + 1)
                    if t >= 2:
                        pe.wait_ge(pt_done, B + t - 1)
                    for k in range(width(qt) // P):
                        ins = tp(ptb[t % 2][:, k * P:(k + 1) * P], prob[:, t % 4, k * P:(k + 1) * P],
                                 ident[:, :])
                    ins.then_inc(tr_done, 1)

                def values(t):
                    p, qt = job(layer, t % J)
                    j = t // J
                    n = width(qt) // P
                    pe.wait_ge(pt_done, B + t + 1)
                    if t >= 2:
                        pe.wait_ge(o_done, B + t - 1)
                    if j >= 1 and t % J < 2:
                        pe.wait_ge(ot_free, 2 * (KT * ATT.index(layer) + j) - 1 + t % J)
                    c0 = (2 * j + p) * HD
                    for k in range(n):
                        ins = mm(obank[t % 2][:, 0:HD], ptsb[:, t % 2, k * P:(k + 1) * P],
                                 vt[:, TOK // P - n + k, c0:c0 + HD], start=k == 0, stop=k == n - 1)
                    ins.then_inc(pv_done, 1)

                def turn_out(j):
                    pe.wait_ge(o_done, B + J * (j + 1))
                    n = J // 4
                    for half in range(2):
                        for k in range(n):
                            ins = mm(obank[half][:, k * P:(k + 1) * P], otok[:, half * n + k, :], flip[:, :],
                                     start=True, stop=True)
                        ins.then_inc(ot_done, 1)

                scores(0)
                scores(1)
                scores(2)
                keep_warm(8)
                for t in range(NJ + 1):
                    if t + 3 < NJ:
                        scores(t + 3)
                    if t < NJ:
                        turn(t)
                    if t % J == 1 and t > J:
                        turn_out(t // J - 1)
                    if t >= 1:
                        values(t - 1)
                turn_out(KT - 1)

            pe.wait_ge(consts, 5)
            pe.wait_ge(small_in, 16 * len(small_parts))
            for t in range(3):
                n = min(P, V_END - t * P)
                ins = tp(ptb[0][:, t * P:t * P + n], stage[0:n, t, :], ident[0:n, 0:n])
            ins.then_inc(vt_done, 1)

            def turn_x(kt):
                if kt >= 4:
                    pe.wait_ge(x_init, kt - 3)
                for tt in range(TOK // P):
                    ins = tp(sbank[kt % 4][:, tt * P:(tt + 1) * P], xtok[:, tt, kt * P:(kt + 1) * P],
                             ident[:, :])
                ins.then_inc(xtr_done, 1)

            def first_ada(g):
                pe.wait_ge(apro_in[g], 16)
                if g >= 2:
                    pe.wait_ge(arow_done, g - 1)
                for kt in range(KT):
                    ins = mm(ptb[g % 2][0:2, :], sc[:, kt, :], apro[g][:, kt, :], start=kt == 0,
                             stop=kt == KT - 1)
                ins.then_inc(apro_done, 1)

            def turn_ada(g):
                pe.wait_ge(arow_done, g + 1)
                for t in range(AG):
                    col = g * AG + t
                    ins = tp(adap[:, col:col + NC + 1:NC], arow[0:2, g % 2, t * P:(t + 1) * P], ident[0:2, 0:2])
                ins.then_inc(arow_out, 1)

            pe.wait_ge(x_in[0], 16)
            pe.wait_ge(x_in[1], 16)
            for kt in range(KT // 2):
                turn_x(kt)
            pe.wait_ge(silu_done, 1)
            first_ada(0)
            for kt in range(KT // 2, KT):
                turn_x(kt)
            first_ada(1)
            turn_ada(0)
            first_ada(2)
            turn_ada(1)
            sum_squares(0)
            first_ada(3)
            turn_ada(2)
            turn_ada(3)

            owed = None
            for ph in phases:
                if ph.name == "wo":
                    pe.wait_ge(ot_free, 2 * KT * (ATT.index(ph.layer) + 1))
                total = ph.units // 2
                cuts = sorted({0, 1, total, min(ph.ada_iters + 1, total)})
                for first, end in zip(cuts, cuts[1:]):
                    def body(i):
                        if first == 0:
                            reduced = owed
                        else:
                            reduced = (ph, i - 1) if first <= ph.ada_iters else None
                        unit(ph, i, 0, first == 0, reduced)
                        unit(ph, i, 1, first == 0)
                    iterate(pe, first, end - first, body)
                owed = (ph, total - 1) if ph.ada_iters == total else None
                if owed and ph.name in ("v", "wo"):
                    reduce_ada(*owed)
                    owed = None
                if ph.name == "v":
                    attention(ph.layer)
                if finals(ph):
                    sum_squares(norm_of(ph))
                    if norm_of(ph) < 2 * DEPTH:
                        keep_warm(26)
            for t in range(SEQ // P):
                for kt in range(KT):
                    if t == 0:
                        pe.wait_ge(t_done, KT * 2 * DEPTH + kt + 1)
                    ins = tp(sbank[2 * t + kt // 4][:, kt % 4 * P:(kt % 4 + 1) * P],
                             fin[:, kt, t * P:(t + 1) * P], ident[:, :])
                ins.then_inc(fin_tr, 1)

        @block.scalar
        def _(act):
            go = nc.scalar.activation

            def split_hi(ph, i, par):
                n = i * 2 + (ph.unit0 + par)
                act.wait_ge(raw_in[par], (i + (ph.unit0 // 2 + 1)) * 16)
                if not (isinstance(i, int) and n < 2):
                    act.wait_ge(pe_done, n - 1)
                go(whi[:, par, 0:ph.slabs, :], raw[:, par, 0:ph.slabs, :], ACT.Copy).then_inc(hi_done, 1)

            def square(r, i, m, n):
                if not (isinstance(i, int) and i == 0):
                    act.wait_ge(acc_done, i * 2 + (7 * r + m))
                elif r:
                    act.wait_ge(ss_done, r)
                go(sq[:, m, 0:n], xT[:, i * 2 + m, 0:n], ACT.Square).then_inc(sq_done, 1)

            def drain(ph, i, par):
                n = ph.tokens
                u = i * 2 + par
                nn = i * 2 + (ph.unit0 + par)
                src = pair[par][:, :, 0:n]
                if ph.name in ("q", "k"):
                    act.wait_ge(pe_done, nn + 1)
                    if ph.name == "k":
                        go(kT[:, bass.ds(u * 2, 2), 0:n], src, ACT.Copy).then_inc(drained[par], 1)
                        return
                    for m in range(2):
                        first = pair[par][:, m, GRID_W - 1:GRID_W]
                        turned = bass.AP(first.tensor, first.offset,
                                         [list(first.ap[0]), [GRID_W, n // GRID_W], [-1, GRID_W]])
                        ins = go(qT[:, u * 2 + m, 0:n].rearrange("p (r c) -> p r c", c=GRID_W), turned,
                                 ACT.Copy, scale=SCALE)
                    ins.then_inc(drained[par], 1)
                elif ph.name == "v":
                    act.wait_ge(pe_done, nn + 1)
                    go(vt[:, :, bass.ds(u * UC, UC)],
                       pair[par][:, :, :].rearrange("p a (b c) -> p (a b) c", c=UC), ACT.Copy)\
                        .then_inc(drained[par], 1)
                elif ph.name == "up" and par == 0:
                    act.wait_ge(pe_done, nn + 1)
                    act.wait_ge(drained[1], i + ph.unit0 // 2)
                    go(gs[:, :, 0:n], src, ACT.Silu).then_inc(drained[par], 1)
                elif ph.name == "conv" and par == 0:
                    act.wait_ge(pe_done, nn + 1)
                    act.wait_ge(drained[1], i + ph.unit0 // 2)
                    go(gs[:, :, 0:n], src, ACT.Copy).then_inc(drained[par], 1)

            def chunk_hi(dst, n, ready, count):
                act.wait_ge(ready, count)
                go(dst, tb[:, :, 0:n], ACT.Copy).then_inc(uhi_done, 1)

            def pool_hi(g):
                chunk_hi(hhi[:, 2 * g:2 * g + 2, :], TOK, tb_ready, g + 1)

            def root(r):
                n = norm_tokens(r)
                act.wait_ge(ss_done, r + 1)
                if r:
                    act.wait_ge(t_done, KT * r)
                go(rstd[:, 0:n], ssp[:, 0:n], ACT.Sqrt, bias=epst[:, 0:1], scale=1.0 / D).then_inc(sd_done, 1)

            def norm(r):
                n = norm_tokens(r)
                layer, mix = r // 2, r % 2 == 0
                if r == 2 * DEPTH:
                    return
                for kt in range(KT):
                    act.wait_ge(t_done, KT * r + kt + 1)
                    for s in range(n // SEQ):
                        bias = modv[:, layer % 2, s, (0 if mix else 3) * KT + kt:(0 if mix else 3) * KT + kt + 1]
                        if mix and layer % 3 == 2:
                            dst = hp[:, 2 * kt + s, PAD:PAD + SEQ]
                        else:
                            dst = hhi[:, kt, cols(s)]
                        ins = go(dst, tr[:, kt % TR, cols(s)], ACT.Identity, bias=bias)
                    ins.then_inc(hh_done, 1)

            def attention(layer):
                J, B = JOBS[layer], JBASE[layer]
                a = ATT.index(layer)

                def exps(j, idx, start):
                    _, qt = job(layer, idx)
                    w = width(qt)
                    t = j * J + (B + idx)
                    act.wait_ge(nm_done, t + 1)
                    if not (start and idx < 4):
                        act.wait_ge(tr_done, t - 3)
                    if not start:
                        act.wait_ge(o_done, t - J + 1)
                    go(prob[:, idx % 4, 0:w], sbank[idx % 4][:, TOK - w:TOK], ACT.Exp,
                       bias=nmx[:, idx:idx + 1], accum_out=rsum[:, idx:idx + 1]).then_inc(p_done, 1)

                def copy_turned(j, idx, start):
                    _, qt = job(layer, idx)
                    t = j * J + (B + idx)
                    act.wait_ge(tr_done, t + 1)
                    if not (start and idx < 2):
                        act.wait_ge(pv_done, t - 1)
                    go(ptsb[:, idx % 2, 0:width(qt)], ptb[idx % 2][:, 0:width(qt)], ACT.Copy)\
                        .then_inc(pt_done, 1)

                def out_hi(j):
                    n = J // 4 * P
                    for half in range(2):
                        act.wait_ge(ot_done, j * 2 + (2 * KT * a + half + 1))
                        go(hhi[:, j, half * n:(half + 1) * n], obank[half][:, 0:n], ACT.Copy)\
                            .then_inc(ot_hi, 1)

                def tile(j, start):
                    for idx in range(J):
                        exps(j, idx, start)
                        if idx:
                            copy_turned(j, idx - 1, start)
                        elif not start:
                            copy_turned(j - 1, J - 1, False)
                        if idx == 1 and not start:
                            out_hi(j - 1)

                tile(0, True)
                with act.Fori(1, KT) as j:
                    tile(j, False)
                copy_turned(KT - 1, J - 1, False)
                out_hi(KT - 1)

            for src, t, r0, n in small_parts:
                act.dma_start(stage[r0:r0 + n, t, :], src).then_inc(small_in, 16)
            act.wait_ge(vt_done, 1)
            go(vecs[:, 0:V_END], ptb[0][:, 0:V_END], ACT.Copy).then_inc(vecs_done, 1)
            act.wait_ge(vecs_done, 1)
            go(sc[:, :, :], vecs[:, V_C:V_END].rearrange("p (s k) -> p k s", s=2), ACT.Silu)\
                .then_inc(silu_done, 1)

            def copy_rows(g):
                act.wait_ge(apro_done, g + 1)
                if g >= 2:
                    act.wait_ge(arow_out, g - 1)
                go(arow[0:2, g % 2, :], ptb[g % 2][0:2, :], ACT.Copy).then_inc(arow_done, 1)

            for kt in range(KT):
                act.wait_ge(x_init, kt + 1)
                square(0, kt // 2, kt % 2, TOK)
                if kt == KT // 2:
                    copy_rows(0)
            copy_rows(1)
            split_hi(phases[0], 0, 0)
            copy_rows(2)
            split_hi(phases[0], 0, 1)
            root(0)
            copy_rows(3)
            norm(0)

            for k, ph in enumerate(phases):
                nxt = following.get(k)
                for first, count, ada, last in sections(ph):
                    def body(i):
                        for par in range(2):
                            drain(ph, i, par)
                            if not last:
                                split_hi(ph, i + 1, par)
                            elif nxt:
                                split_hi(nxt, 0, par)
                            if ph.name == "pool" and not last:
                                pool_hi(i * 2 + par + 2)
                            if ph.name == "up" and par == 1:
                                chunk_hi(uhi[:, bass.ds(i * 2, 2), 0:ph.tokens], ph.tokens,
                                         drained[1], i + (ph.unit0 // 2 + 1))
                            if ph.name == "gateb":
                                chunk_hi(yhi[:, bass.ds((i * 2 + par) * 2, 2), 0:ph.tokens], ph.tokens,
                                         drained[par], i + (ph.unit0 // 2 + 1))
                            if finals(ph):
                                if ph.name != "down":
                                    q = i * 2 + par
                                elif par == 1:
                                    q = i
                                else:
                                    continue
                                r = norm_of(ph)
                                act.wait_ge(xt_done, q + pair_base(r) + 1)
                                square(r, q, 0, ph.tokens)
                                act.wait_ge(drained[par], i + (ph.unit0 // 2 + 1))
                                square(r, q, 1, ph.tokens)
                    iterate(act, first, count, body)
                if ph.name == "v":
                    attention(ph.layer)
                if finals(ph):
                    r = norm_of(ph)
                    root(r)
                    norm(r)
                    if pools(r):
                        for g in range(2):
                            pool_hi(g)
            for t in range(SEQ // P):
                act.wait_ge(fin_tr, t + 1)
                for b in range(2):
                    go(fout[:, t, b * 512:(b + 1) * 512], sbank[2 * t + b], ACT.Copy).then_inc(fin_ev, 1)

        @block.vector
        def _(dve):
            links = [0]

            def link(ins):
                links[0] += 1
                ins.then_inc(chain_s, 1)
                dve.wait_ge(chain_s, links[0])

            tt, ts, stt = nc.vector.tensor_tensor, nc.vector.tensor_scalar, nc.vector.scalar_tensor_tensor

            def split_lo(ph, i, par):
                n = i * 2 + (ph.unit0 + par)
                dve.wait_ge(hi_done, n + 1)
                tt(wlo[:, par, 0:ph.slabs, :], raw[:, par, 0:ph.slabs, :],
                   whi[:, par, 0:ph.slabs, :].bitcast(F32), ALU.subtract).then_inc(lo_done, 1)

            def ada(ph, i, par):
                a = i * 2 + (ph.ada_unit0 + par)
                dve.wait_ge(ada_in[par], (i + (ph.ada_unit0 // 2 + 1)) * 16)
                if par == 0 and not (isinstance(i, int) and a < 2):
                    dve.wait_ge(ada_reduced, i + ph.ada_unit0 // 2)
                for k in range(4):
                    for s in range(2):
                        o = 2 * k + s
                        src = araw[:, par, k, :]
                        w = sc[:, 4 * par + k, s:s + 1]
                        if par == 0 and k == 0:
                            ins = ts(acc[:, s, :], src, w, None, ALU.mult)
                        else:
                            dve.wait_ge(ada_ops, a * 8 + (o - 1))
                            ins = stt(out=acc[:, s, :], in0=src, scalar=w, in1=acc[:, s, :],
                                      op0=ALU.mult, op1=ALU.add)
                        ins.then_inc(ada_ops, 1)

            def take_mod(layer, part0, part1, extra=None):
                c0, c1 = part0 * KT, part1 * KT
                for s in range(2):
                    ins = tt(modv[:, layer % 2, s, c0:c1], adap[:, s * NC + c0:s * NC + c1],
                             vecs[:, V_B + layer * NC + c0:V_B + layer * NC + c1], ALU.add)
                link(ins)

            def chunk_lo(chunk, hi, lo, n):
                dve.wait_ge(uhi_done, chunk + 1)
                tt(lo, tb[:, :, 0:n], hi.bitcast(F32), ALU.subtract).then_inc(u_done, 1)

            def residual(ph, i, par, q, last_sum):
                part = 5 if ph.name == "down" else 2
                for m in range(2):
                    for s in range(ph.tokens // SEQ):
                        xa = xT[:, q * 2 + m, cols(s)]
                        if ph.name == "pool":
                            gate = pgate[:, s, bass.ds(q * 2 + m, 1)]
                        else:
                            gate = modv[:, ph.layer % 2, s, bass.ds(q * 2 + (part * KT + m), 1)]
                        ins = stt(out=xa, in0=pair[par][:, m, cols(s)], scalar=gate, in1=xa,
                                  op0=ALU.mult, op1=ALU.add)
                    if last_sum and m == 0:
                        ins.then_inc(xt_done, 1)
                ins.then_inc(drained[par], 1)

            def add_squares(r, q, n):
                for m in range(2):
                    dve.wait_ge(sq_done, q * 2 + (KT * r + m + 1))
                    dve.wait_ge(acc_done, q * 2 + (7 * r + m + 1))
                    tt(acc2[:, m, 0:n], acc2[:, m, 0:n], sq[:, m, 0:n], ALU.add).then_inc(acc_done, 1)

            def start_squares(r):
                if r:
                    dve.wait_ge(ss_done, r)
                nc.vector.memset(acc2[:, :, :], 0.0).then_inc(acc_done, 1)

            def scales(r):
                if r == 2 * DEPTH:
                    return
                layer, mix = r // 2, r % 2 == 0
                v0 = (V_GM if mix else V_GF) + layer * KT
                p0 = (1 if mix else 4) * KT
                for s in range(norm_tokens(r) // SEQ):
                    ins = stt(out=moda[:, s, :], in0=modv[:, layer % 2, s, p0:p0 + KT], scalar=1.0,
                              in1=vecs[:, v0:v0 + KT], op0=ALU.add, op1=ALU.mult)
                link(ins)

            def reciprocal(r):
                n = norm_tokens(r)
                dve.wait_ge(sd_done, r + 1)
                link(nc.vector.reciprocal(rstd[:, 0:n], rstd[:, 0:n]))

            def norm(r):
                n = norm_tokens(r)
                layer, mix = r // 2, r % 2 == 0
                streams = n // SEQ

                def tr_free(kt):
                    if kt >= TR and pools(r):
                        dve.wait_ge(hh_done, KT * r + kt - TR + 1)
                    elif kt >= TR and r < 2 * DEPTH:
                        dve.wait_ge(h_done, h_base(r) + kt - TR + 1)

                def scaled(kt):
                    tr_free(kt)
                    for s in range(streams):
                        a = vecs[:, V_FG + kt:V_FG + kt + 1] if r == 2 * DEPTH else moda[:, s, kt:kt + 1]
                        dst = fin[:, kt, :] if r == 2 * DEPTH else tr[:, kt % TR, cols(s)]
                        ins = stt(out=dst, in0=xT[:, kt, cols(s)], scalar=a, in1=rstd[:, cols(s)],
                                  op0=ALU.mult, op1=ALU.mult)
                    ins.then_inc(t_done, 1)

                def low(kt):
                    dve.wait_ge(hh_done, KT * r + kt + 1)
                    if mix and layer % 3 == 2:
                        return
                    for s in range(streams):
                        c0 = (0 if mix else 3) * KT + kt
                        ins = stt(out=hlo[:, kt, cols(s)], in0=tr[:, kt % TR, cols(s)],
                                  scalar=modv[:, layer % 2, s, c0:c0 + 1],
                                  in1=hhi[:, kt, cols(s)].bitcast(F32), op0=ALU.add, op1=ALU.subtract)
                    ins.then_inc(h_done, 1)

                for kt in range(KT + 1):
                    if kt < KT:
                        scaled(kt)
                    if kt and r < 2 * DEPTH:
                        low(kt - 1)

            def pooled_tiles(ph, g):
                win = POOL_WINDOWS[g]
                hw = win // 2
                if g == len(POOL_WINDOWS) - 1:
                    dve.wait_ge(sums_ready, 1)
                else:
                    link(window_sums(g, nc.vector, link))
                sums = pw[:, 2 if g == len(POOL_WINDOWS) - 1 else g % 2, g % 2, :, PAD:PAD + SEQ]
                for c0, n in ((0, hw), (SEQ - hw + 1, hw - 1)):
                    if n:
                        e0 = 0 if c0 == 0 else 2 * PAD - n
                        ins = tt(sums[:, :, c0:c0 + n], sums[:, :, c0:c0 + n],
                                 ratio[:, g, e0:e0 + n].unsqueeze(1).to_broadcast([P, 4, n]), ALU.mult)
                link(ins)
                dve.wait_ge(u_done, ph.chunk0 + g)
                stt(out=tb[:, :, :].rearrange("p m (s t) -> p (m s) t", s=2), in0=sums, scalar=1.0 / win,
                    in1=hp[:, 4 * g:4 * g + 4, PAD:PAD + SEQ], op0=ALU.mult, op1=ALU.subtract)\
                    .then_inc(tb_ready, 1)
                chunk_lo(ph.chunk0 + g, hhi[:, 2 * g:2 * g + 2, :], hlo[:, 2 * g:2 * g + 2, :], TOK)

            def attention(layer):
                J, B = JOBS[layer], JBASE[layer]
                a = ATT.index(layer)

                def maxima(j, idx):
                    p, qt = job(layer, idx)
                    t = j * J + (B + idx)
                    s = sbank[idx % 4]
                    dve.wait_ge(s_done, t + 1)
                    if width(qt) == TOK:
                        dve.wait_ge(bias_ready, j * 2 + (a * HEADS + p + 1))
                    ins = nc.vector.reduce_max(mx[:, 1, idx:idx + 1], s[:, SEQ:TOK], AXX)
                    if width(qt) == TOK:
                        ins = nc.vector.tensor_tensor_reduce(s[:, 0:SEQ], s[:, 0:SEQ], biasm[:, p, qt, :], 1.0,
                                                             -BIG, ALU.add, ALU.max, mx[:, 0, idx:idx + 1])
                    ins.then_inc(mx_done, 1)
                    dve.wait_ge(mx_done, t + 1)
                    if width(qt) == TOK:
                        ins = ts(nmx[:, idx:idx + 1], mx[:, 0, idx:idx + 1], mx[:, 1, idx:idx + 1], -1.0,
                                 ALU.max, ALU.mult)
                    else:
                        ins = ts(nmx[:, idx:idx + 1], mx[:, 1, idx:idx + 1], -1.0, None, ALU.mult)
                    ins.then_inc(nm_done, 1)

                def normalise(j, idx, start):
                    p, qt = job(layer, idx)
                    t = j * J + (B + idx)
                    dve.wait_ge(pv_done, t + 1)
                    nc.vector.reciprocal(rinv[:, idx:idx + 1], rsum[:, idx:idx + 1]).then_inc(ri_done, 1)
                    dve.wait_ge(ri_done, t + 1)
                    if idx == 0 and not start:
                        dve.wait_ge(ot_done, j * 2 + 2 * KT * a)
                    ts(otok[:, qt, p * HD:(p + 1) * HD], obank[idx % 2][:, 0:HD], rinv[:, idx:idx + 1], None,
                       ALU.mult).then_inc(o_done, 1)

                def out_lo(j):
                    n = J // 4 * P
                    for half in range(2):
                        dve.wait_ge(ot_hi, j * 2 + (2 * KT * a + half + 1))
                        c0 = half * n
                        tt(hlo[:, j, c0:c0 + n], obank[half][:, 0:n], hhi[:, j, c0:c0 + n].bitcast(F32),
                           ALU.subtract).then_inc(ot_free, 1)

                def tile(j, start):
                    for idx in range(J):
                        maxima(j, idx)
                        if idx == 3 and not start:
                            out_lo(j - 1)
                        if idx >= 3:
                            normalise(j, idx - 3, start)
                        elif not start:
                            normalise(j - 1, J - 3 + idx, False)

                tile(0, True)
                with dve.Fori(1, KT) as j:
                    tile(j, False)
                normalise(KT - 1, J - 3, False)
                normalise(KT - 1, J - 2, False)
                normalise(KT - 1, J - 1, False)
                out_lo(KT - 1)

            def drain(ph, i, par):
                n = ph.tokens
                nn = i * 2 + (ph.unit0 + par)
                if ph.name == "up" and par == 1:
                    dve.wait_ge(drained[0], i + (ph.unit0 // 2 + 1))
                    if not (isinstance(i, int) and i + ph.chunk0 == 0):
                        dve.wait_ge(u_done, i + ph.chunk0)
                    dve.wait_ge(pe_done, nn + 1)
                    tt(tb[:, :, 0:n], gs[:, :, 0:n], pair[1][:, :, 0:n], ALU.mult).then_inc(drained[1], 1)
                elif ph.name == "gateb":
                    dve.wait_ge(conv_ops, 6 * KT // 2)
                    dve.wait_ge(u_done, i * 2 + (ph.chunk0 + par))
                    dve.wait_ge(pe_done, nn + 1)
                    tt(tb[:, :, 0:n], cv[:, bass.ds((i * 2 + par) * 2, 2), 0:n], pair[par][:, :, 0:n], ALU.mult)\
                        .then_inc(drained[par], 1)
                elif ph.name == "conv" and par == 1:
                    dve.wait_ge(drained[0], i + (ph.unit0 // 2 + 1))
                    dve.wait_ge(pe_done, nn + 1)
                    if not (isinstance(i, int) and i == 0):
                        dve.wait_ge(conv_ops, i * 6)
                    tt(tb[:, :, 0:n], gs[:, :, 0:n], pair[1][:, :, 0:n], ALU.mult).then_inc(drained[1], 1)
                    dve.wait_ge(drained[1], i + (ph.unit0 // 2 + 1))
                    o = 0
                    for tap, (d0, s0) in ((1, (0, 0)), (0, (1, 0)), (2, (0, 1))):
                        w = SEQ - (tap != 1)
                        for m in range(2):
                            dst = cv[:, i * 2 + m, :].rearrange("p (s t) -> p s t", s=2)[:, :, d0:d0 + w]
                            src = tb[:, m, :].rearrange("p (s t) -> p s t", s=2)[:, :, s0:s0 + w]
                            wt = vecs[:, bass.ds(i * 2 + (V_CW + tap * KT + m), 1)]
                            if tap == 1:
                                ins = ts(dst, src, wt, None, ALU.mult)
                            else:
                                dve.wait_ge(conv_ops, i * 6 + (o - 1))
                                ins = stt(out=dst, in0=src, scalar=wt, in1=dst, op0=ALU.mult, op1=ALU.add)
                            ins.then_inc(conv_ops, 1)
                            o += 1
                elif ph.name in ("wo", "scout", "pool"):
                    dve.wait_ge(pe_done, nn + 1)
                    residual(ph, i, par, i * 2 + par, True)
                elif ph.name == "down":
                    dve.wait_ge(pe_done, nn + 1)
                    dve.wait_ge(drained[1 - par], i + (ph.unit0 // 2 + par))
                    residual(ph, i, par, i, par == 1 and finals(ph))

            start_squares(0)
            for kt in range(KT):
                dve.wait_ge(xtr_done, kt + 1)
                nc.vector.tensor_copy(xT[:, kt, :], sbank[kt % 4]).then_inc(x_init, 1)
                if kt % 2 and kt < KT - 1:
                    add_squares(0, kt // 2, TOK)
            split_lo(phases[0], 0, 0)
            split_lo(phases[0], 0, 1)
            reciprocal(0)
            dve.wait_ge(vecs_done, 1)
            dve.wait_ge(arow_out, PG)
            take_mod(0, 0, 2)
            scales(0)
            norm(0)

            for k, ph in enumerate(phases):
                nxt = following.get(k)
                if finals(ph):
                    start_squares(norm_of(ph))
                if ph.name == "down" and ph.tile0 and ph.layer < DEPTH - 1:
                    dve.wait_ge(ada_reduced, ph.ada_unit0 // 2)
                    take_mod(ph.layer + 1, 0, N_MOD)
                for first, count, with_ada, last in sections(ph):
                    def body(i):
                        for par in range(2):
                            if with_ada:
                                ada(ph, i, par)
                            drain(ph, i, par)
                            if ph.name == "gateb":
                                q = i * 2 + par
                                t = bass.ds(q * 2, 2)
                            if not last:
                                split_lo(ph, i + 1, par)
                            elif nxt:
                                split_lo(nxt, 0, par)
                            if ph.name == "pool" and not last:
                                pooled_tiles(ph, i * 2 + par + 2)
                            if ph.name == "up" and par == 1:
                                t = bass.ds(i * 2, 2)
                                chunk_lo(i + ph.chunk0, uhi[:, t, 0:ph.tokens], ulo[:, t, 0:ph.tokens], ph.tokens)
                            if ph.name == "gateb":
                                chunk_lo(q + ph.chunk0, yhi[:, t, :], ylo[:, t, :], ph.tokens)
                            if finals(ph):
                                if ph.name != "down":
                                    if not (last and par == 1):
                                        add_squares(norm_of(ph), i * 2 + par, ph.tokens)
                                elif par == 1 and not last:
                                    add_squares(norm_of(ph), i, ph.tokens)
                    iterate(dve, first, count, body)
                if ph.name == "v":
                    if ph.ada_iters:
                        dve.wait_ge(ada_reduced, ph.ada_unit0 // 2 + ph.ada_iters)
                        take_mod(0, 2, 5)
                    attention(ph.layer)
                if ph.name == "wo" and ph.ada_iters:
                    dve.wait_ge(ada_reduced, ph.ada_unit0 // 2 + ph.ada_iters)
                    take_mod(0, 5, 6)
                if finals(ph):
                    r = norm_of(ph)
                    pooled = pools(r)
                    if pooled:
                        nl = r // 2
                        for s in range(2):
                            ins = tt(pgate[:, s, :], modv[:, nl % 2, s, 2 * KT:3 * KT],
                                     vecs[:, V_PS:V_PS + KT], ALU.mult)
                        nc.vector.memset(hp[:, :, 0:PAD], 0.0)
                        nc.vector.memset(hp[:, :, PAD + SEQ:PW], 0.0).then_inc(pads_ready, 1)
                    scales(r)
                    reciprocal(r)
                    norm(r)
                    if pooled:
                        pooled_tiles(following[k], 0)
                        pooled_tiles(following[k], 1)


_INS = ["x", "c", "ctx", "c_ctx", "adaln_w", "adaln_b", "norm_mix_g", "norm_ffn_g", "ffn_w1", "ffn_w3",
        "ffn_w2", "na_w_qkv", "na_w_o", "na_rpb", "sc_w_in", "sc_conv_w", "sc_w_out", "pool_w",
        "pool_scale", "final_g"]


def kernel(**inputs):
    import numpy as _np
    import concourse.bacc as _bacc
    from concourse import mybir as _mybir
    from concourse.bass_utils import run_bass_kernel_spmd as _run

    nc = _bacc.Bacc("TRN2", target_bir_lowering=False, num_devices=1)
    arrays, args = {}, []
    for name in _INS:
        a = _np.ascontiguousarray(inputs[name])
        arrays[f"in_{name}_dram"] = a
        args.append(nc.dram_tensor(f"in_{name}_dram", a.shape, _mybir.dt.from_np(a.dtype), kind="ExternalInput").ap())
    shape = inputs["x"].shape
    args.append(nc.dram_tensor("out_0_dram", shape, _mybir.dt.float32, kind="ExternalOutput").ap())
    build(nc, *args)
    r = _run(nc, [arrays], core_ids=[0])
    return r.results[0]["out_0_dram"]
```

```python
from contextlib import ExitStack
from typing import NamedTuple

import numpy as np

import concourse.bass as bass
from concourse import mybir

F32 = mybir.dt.float32
F32R = mybir.dt.float32r
ALU = mybir.AluOpType
ACT = mybir.ActivationFunctionType
AXX = mybir.AxisListType.X

P = 128
EPS = 1e-6
GRID_W = 64
WIN_W = 16
CONV_W = 3
POOL_WINDOWS = (2, 4, 8, 16)
N_MOD = 6
BIG = 3.0e38
UC = 256
AC = 512
PAD = 8


class Phase(NamedTuple):
    name: str
    layer: int
    units: int
    slabs: int
    tokens: int
    unit0: int
    fresh: bool = False
    ada_from: int = 0
    ada_to: int = 0
    ada_layer: int = 0
    ada_group: int = 0
    ada_unit0: int = 0
    chunk0: int = 0
    tile0: int = 0


def sections(ph):
    total = ph.units // 2
    cuts = sorted({0, ph.ada_from, ph.ada_to, total - 1, total})
    for a, b in zip(cuts, cuts[1:]):
        yield a, b - a, ph.ada_from <= a < ph.ada_to, a == total - 1


def iterate(eng, first, count, body):
    if count == 1:
        body(first)
    else:
        with eng.Fori(first, first + count) as i:
            body(i)


def plan(kt, ff_tiles, depth, n_tok, n_lat):
    phases = []
    counts = {"unit": 0, "ada": 0, "chunk": 0}
    groups = N_MOD * kt * P // AC

    def add(name, layer, units, slabs, tokens, ada_iters=0, ada_layer=0, ada_group=0, chunks=0,
            ada_from=0, **kw):
        ada_from = ada_from if ada_iters else 0
        phases.append(Phase(name, layer, units, slabs, tokens, counts["unit"], ada_from=ada_from,
                            ada_to=ada_from + ada_iters, ada_layer=ada_layer,
                            ada_group=ada_group - ada_from, ada_unit0=counts["ada"] - 2 * ada_from,
                            chunk0=counts["chunk"], **kw))
        counts["unit"] += units
        counts["ada"] += 2 * ada_iters
        counts["chunk"] += chunks

    wide = kt * P // UC
    half = (ff_tiles // 2 + 1) // 2 * 2
    for layer in range(depth):
        kind = layer % 3
        last = layer == depth - 1
        tok = n_lat if last else n_tok
        own = 2 if layer == 0 else 0
        if kind == 0:
            add("k", layer, wide, kt, n_tok, fresh=True, ada_iters=own, ada_group=4)
            add("q", layer, wide, kt, tok, ada_iters=own, ada_group=6)
            add("v", layer, wide, kt, n_tok, ada_iters=own, ada_group=8)
            add("wo", layer, wide, kt, tok, ada_iters=own, ada_group=10)
        elif kind == 1:
            add("conv", layer, 2 * wide, kt, tok, fresh=True)
            add("gateb", layer, wide, kt, tok, chunks=wide)
            add("scout", layer, wide, kt, tok)
        else:
            add("pool", layer, len(POOL_WINDOWS), kt // len(POOL_WINDOWS), tok, chunks=wide)
        nxt = 0 if last else 1
        tiles = (half, ff_tiles - half)
        per = [nxt * (tiles[0] // 2 - 1), nxt * 2]
        per.append(nxt * (groups - sum(per)))
        add("up", layer, tiles[0], kt, tok, per[0], layer + 1, 0, tiles[0] // 2, fresh=True,
            ada_from=1)
        add("down", layer, 2 * wide, tiles[0] // 2, tok, per[1], layer + 1, per[0])
        add("up", layer, tiles[1], kt, tok, per[2], layer + 1, per[0] + per[1], tiles[1] // 2,
            tile0=tiles[0])
        add("down", layer, 2 * wide, tiles[1] // 2, tok, tile0=tiles[0])
    return phases


def build(nc, x, c, ctx, c_ctx, adaln_w, adaln_b, norm_mix_g, norm_ffn_g, ffn_w1, ffn_w3, ffn_w2,
          na_w_qkv, na_w_o, na_rpb, sc_w_in, sc_conv_w, sc_w_out, pool_w, pool_scale, final_g, out):
    _, SEQ, D = x.shape
    CTX = ctx.shape[1]
    DEPTH = adaln_w.shape[0]
    FF = ffn_w1.shape[2]
    HEADS, DR, DC = na_rpb.shape[1:]
    KT = D // P
    TOK = SEQ + CTX
    ROWS = SEQ // GRID_W
    HD = D // HEADS
    SCALE = float(HD) ** -0.5
    FT = FF // P
    NC = N_MOD * KT
    AG = AC // P
    assert (SEQ, CTX, HD, DEPTH, DR // 2 + 1) == (256, 256, 64, 4, 8) and ROWS <= 8 and FF % UC == 0

    phases = plan(KT, FT, DEPTH, TOK, SEQ)
    following = dict(zip(range(len(phases)), phases[1:]))
    HALF = phases[[p.name for p in phases].index("up")].units

    place = [(nc.sbuf_base + 63) // 64 * 64]

    def at(name, shape, dt, offset):
        return nc.alloc_sbuf_tensor_at(name, [P] + shape, dt, offset=offset)

    def new(name, shape, dt=F32):
        t = at(name, shape, dt, place[0])
        place[0] += (int(np.prod(shape)) * 4 + 63) // 64 * 64
        return t

    xT = new("xT", [KT, TOK])
    hhi = new("hhi", [KT, TOK], F32R)
    hlo_at = place[0]
    hlo = new("hlo", [KT, TOK], F32R)
    raw = new("raw", [2, 8, UC])
    whi = new("whi", [2, 8, UC], F32R)
    wlo = new("wlo", [2, 8, UC], F32R)
    araw_at = place[0]
    araw = new("araw", [2, 4, AC])
    acc = new("acc", [2, AC])
    u_at = place[0]
    uhi = new("uhi", [HALF, TOK], F32R)
    ulo = new("ulo", [HALF, TOK], F32R)
    qT = at("qT", [KT, TOK], F32, u_at)
    kT = at("kT", [KT, TOK], F32, u_at + KT * TOK * 4)
    vt = at("vt", [TOK // P, D], F32, u_at + 2 * KT * TOK * 4)
    yhi = at("yhi", [KT, TOK], F32R, u_at)
    ylo = at("ylo", [KT, TOK], F32R, u_at + KT * TOK * 4)
    cv = at("cv", [KT, TOK], F32, u_at + 2 * KT * TOK * 4)
    PW = SEQ + 2 * PAD
    hp = at("hp", [KT * 2, PW], F32, u_at)
    pw = at("pw", [3, 2, 4, PW], F32, u_at + KT * 2 * PW * 4)
    fin = at("fin", [KT, SEQ], F32, u_at)
    fout = at("fout", [SEQ // P, D], F32, u_at + KT * SEQ * 4)
    PG = 2 * D // AC
    DVE_GROUP = 1
    PE_GROUPS = [g for g in range(PG) if g != DVE_GROUP]
    apro = [at(f"apro{g}", [KT, AC], F32, u_at + g * KT * AC * 4) for g in range(PG - 1)]
    apro += [at(f"apro{PG - 1}", [KT, AC], F32, araw_at)]
    xtok = at("xtok", [TOK // P, D], F32, hlo_at)
    work_at = place[0]
    TR = 6
    gs = new("gs", [2, TOK])
    tb = new("tb", [2, TOK])
    sq = new("sq", [2, TOK])
    acc2 = new("acc2", [2, TOK])
    rstd = new("rstd", [TOK])
    tr = new("tr", [TR, SEQ])
    prob = at("prob", [4, TOK], F32, work_at)
    ptsb = at("ptsb", [2, TOK], F32, work_at + 4 * TOK * 4)
    otok = at("otok", [TOK // P, P], F32, work_at + 6 * TOK * 4)
    stage = at("stage", [3, P], F32, work_at)
    arow = at("arow", [2, AC], F32, work_at + 2 * TOK * 4)
    braw = new("braw", [2, 2, ROWS * GRID_W])
    biasm = new("biasm", [2, 2, ROWS * GRID_W])
    ones = new("ones", [P])
    ident = new("ident", [P])
    flip = new("flip", [P])
    mask = new("mask", [GRID_W])
    ratio = new("ratio", [len(POOL_WINDOWS), 2 * PAD])
    vecs = new("vecs", [3 * P])
    sc = new("sc", [KT, 2])
    modv = new("modv", [2, 2, NC])
    moda = new("moda", [2, KT])
    pgate = new("pgate", [2, KT])
    epst = new("epst", [1])
    preload = new("preload", [len(phases)])
    nmx = new("nmx", [8])
    mx = new("mx", [2, 8])
    rsum = new("rsum", [8])
    rinv = new("rinv", [8])
    assert place[0] <= nc.sbuf_usable_end, place[0]

    pair = [nc.alloc_psum_tensor(f"pair{p}", [P, 2, 512], F32) for p in range(2)]
    sbank = [pair[0][:, 0, :], pair[0][:, 1, :], pair[1][:, 0, :], pair[1][:, 1, :]]
    ptb = [nc.alloc_psum_tensor(f"ptb{p}", [P, 512], F32) for p in range(2)]
    adap = nc.alloc_psum_tensor("adap", [P, 512], F32)
    ssp = nc.alloc_psum_tensor("ssp", [P, 512], F32)
    obank = [adap, ssp]
    ssb = [ssp[:, 0:SEQ], adap[:, SEQ:2 * SEQ]]
    psP = [pair[p][:, :, :] for p in range(2)]

    V_B = 0
    V_GM = DEPTH * NC
    V_GF = V_GM + DEPTH * KT
    V_CW = V_GF + DEPTH * KT
    V_PS = V_CW + CONV_W * KT
    V_FG = V_PS + KT
    V_C = V_FG + KT
    V_END = V_C + 2 * KT
    small = [
        (adaln_b.rearrange("l (n p) -> (l n) p", p=P), V_B),
        (norm_mix_g.rearrange("l (n p) -> (l n) p", p=P), V_GM),
        (norm_ffn_g.rearrange("l (n p) -> (l n) p", p=P), V_GF),
        (sc_conv_w[0].rearrange("l (n p) -> (l n) p", p=P), V_CW),
        (pool_scale.rearrange("l (n p) -> (l n) p", p=P), V_PS),
        (final_g.rearrange("(n p) -> n p", p=P), V_FG),
        (c.rearrange("l (n p) -> (l n) p", p=P), V_C),
        (c_ctx.rearrange("(n p) -> n p", p=P), V_C + KT),
    ]
    small_parts = []
    for src, col in small:
        r = 0
        while r < src.shape[0]:
            n = min(src.shape[0] - r, P - (col + r) % P)
            small_parts.append((src[r:r + n, :], (col + r) // P, (col + r) % P, n))
            r += n

    def sem(name):
        return nc.alloc_semaphore(name)

    raw_in = [sem("raw_in0"), sem("raw_in1")]
    ada_in = [sem("ada_in0"), sem("ada_in1")]
    hi_done, lo_done, pe_done = sem("hi_done"), sem("lo_done"), sem("pe_done")
    drained = [sem("drained0"), sem("drained1")]
    ada_ops, ada_reduced = sem("ada_ops"), sem("ada_reduced")
    gs_ready, tb_ready, uhi_done, u_done = sem("gs_ready"), sem("tb_ready"), sem("uhi_done"), sem("u_done")
    conv_ops = sem("conv_ops")
    xt_done, sq_done, acc_done, ss_done, sd_done = (sem("xt_done"), sem("sq_done"), sem("acc_done"),
                                                     sem("ss_done"), sem("sd_done"))
    half_done = sem("half_done")
    t_done, hh_done, h_done = sem("t_done"), sem("hh_done"), sem("h_done")
    chain_s = sem("dve_chain")
    s_done, mx_done, nm_done, p_done = sem("s_done"), sem("mx_done"), sem("nm_done"), sem("p_done")
    tr_done, pt_done, pv_done, ri_done, o_done = (sem("tr_done"), sem("pt_done"), sem("pv_done"),
                                                  sem("ri_done"), sem("o_done"))
    ot_done, ot_hi, ot_free = sem("ot_done"), sem("ot_hi"), sem("ot_free")
    bias_in = [sem("bias_in0"), sem("bias_in1")]
    bias_ready = sem("bias_ready")
    small_in, x_in = sem("small_in"), [sem("x_in0"), sem("x_in1")]
    apro_in = [sem(f"apro_in{g}") for g in range(PG)]
    arow_done, arow_out, pro_ops = sem("arow_done"), sem("arow_out"), sem("pro_ops")
    pool_c, consts = sem("pool_chain"), sem("consts")
    vt_done, vecs_done, silu_done, apro_done = sem("vt_done"), sem("vecs_done"), sem("silu_done"), sem("apro_done")
    xtr_done, x_init = sem("xtr_done"), sem("x_init")
    pads_ready, sums_ready = sem("pads_ready"), sem("sums_ready")
    fin_tr, fin_ev, stored = sem("fin_tr"), sem("fin_ev"), sem("stored")

    def norm_tokens(r):
        return SEQ if r >= 2 * DEPTH - 1 else TOK

    ATT = [layer for layer in range(DEPTH) if layer % 3 == 0]
    JOBS = {layer: (2 * SEQ // P if layer == DEPTH - 1 else 2 * TOK // P) for layer in ATT}
    JBASE = {layer: sum(KT * JOBS[m] for m in ATT if m < layer) for layer in ATT}

    def job(layer, idx):
        per = JOBS[layer] // 2
        return idx // per, idx % per

    def width(qt):
        return TOK if qt < SEQ // P else CTX

    def finals(ph):
        return ph.name in ("wo", "scout", "pool") or (ph.name == "down" and ph.tile0 > 0)

    def norm_of(ph):
        return 2 * ph.layer + (2 if ph.name == "down" else 1)

    def pair_base(r):
        return (KT // 2) * (r - 1)

    def streams(r):
        return norm_tokens(r) // SEQ

    def stream_base(r):
        return sum(streams(q) for q in range(r))

    def h_base(r):
        return KT * sum(streams(q) for q in range(r) if not pools(q))

    def pools(r):
        return r % 2 == 0 and (r // 2) % 3 == 2 and r < 2 * DEPTH

    def cols(s):
        return slice(s * SEQ, (s + 1) * SEQ)

    def ada_src(layer, group, half):
        v = adaln_w[layer].rearrange("(k p) n -> p k n", p=P)
        return v[:, 4 * half:4 * half + 4, bass.ds(group * AC, AC)]

    def weight_src(ph, i, par):
        att = ph.layer // 3
        u = i * 2 + par
        rows = "(k p) n -> p k n"
        if ph.name in "qkv":
            return na_w_qkv[att].rearrange(rows, p=P)[:, :, bass.ds(u * UC + "qkv".index(ph.name) * D, UC)]
        if ph.name == "wo":
            return na_w_o[att].rearrange(rows, p=P)[:, :, bass.ds(u * UC, UC)]
        if ph.name == "conv":
            return sc_w_in[0].rearrange(rows, p=P)[:, :, bass.ds(i * UC + (1 + par) * D, UC)]
        if ph.name == "gateb":
            return sc_w_in[0].rearrange(rows, p=P)[:, :, bass.ds(u * UC, UC)]
        if ph.name == "scout":
            return sc_w_out[0].rearrange(rows, p=P)[:, :, bass.ds(u * UC, UC)]
        if ph.name == "pool":
            return pool_w[0, u].rearrange(rows, p=P)
        if ph.name == "up":
            w = (ffn_w1, ffn_w3)[par][ph.layer]
            return w.rearrange(rows, p=P)[:, :, bass.ds(i * UC + ph.tile0 * P, UC)]
        k0 = ph.tile0 + par * ph.slabs
        return ffn_w2[ph.layer].rearrange(rows, p=P)[:, k0:k0 + ph.slabs, bass.ds(i * UC, UC)]

    def window_sums(g, eng, link):
        src, lo, hi, step, k = hp[:, 4 * g:4 * g + 4, :], 0, PW, 1, 0
        ins = None
        while 2 * step <= POOL_WINDOWS[g]:
            if ins:
                link(ins)
            dst = pw[:, 2 if g == len(POOL_WINDOWS) - 1 else g % 2, k % 2, :, :]
            back, fwd = (1, 0) if step == 1 else (step // 2, step // 2)
            lo, hi = lo + back, hi - fwd
            ins = eng.tensor_tensor(dst[:, :, lo:hi], src[:, :, lo - back:hi - back],
                                    src[:, :, lo + fwd:hi + fwd], ALU.add)
            src, step, k = dst, 2 * step, k + 1
        return ins

    with nc.Block() as block:
        @block.sync
        def _(sp):
            def load(ph, i, par):
                n = i * 2 + (ph.unit0 + par)
                if not (isinstance(i, int) and n < 2):
                    sp.wait_ge(lo_done, n - 1)
                sp.dma_start(raw[:, par, 0:ph.slabs, :], weight_src(ph, i, par)).then_inc(raw_in[par], 16)

            def load_ada(ph, i, par):
                a = i * 2 + (ph.ada_unit0 + par)
                if not (isinstance(i, int) and a < 2):
                    sp.wait_ge(ada_ops, a * 8 - 8)
                elif a < 2:
                    sp.wait_ge(apro_done, PG - 1)
                sp.dma_start(araw[:, par, :, :], ada_src(ph.ada_layer, i + ph.ada_group, par))\
                    .then_inc(ada_in[par], 16)

            x_v = x[0].rearrange("(t p) d -> p t d", p=P)
            ctx_v = ctx[0].rearrange("(t p) d -> p t d", p=P)
            ts = SEQ // P
            sp.dma_start(xtok[:, 0:ts, :], x_v).then_inc(x_in[0], 16)
            sp.dma_start(xtok[:, ts:TOK // P, :], ctx_v).then_inc(x_in[1], 16)
            sp.wait_ge(small_in, 16 * len(small_parts))
            for g in range(PG):
                src = adaln_w[0].rearrange("(k p) n -> p k n", p=P)[:, :, g * AC:(g + 1) * AC]
                sp.dma_start(apro[g][:, :, :], src).then_inc(apro_in[g], 16)
            load(phases[0], 0, 0)
            load(phases[0], 0, 1)

            def biases(layer):
                a = ATT.index(layer)
                for h in range(HEADS):
                    if a or h >= 2:
                        sp.wait_ge(bias_ready, a * HEADS + h - 1)
                    for rq in range(ROWS):
                        r0 = rq % 2 * GRID_W
                        off = (a * HEADS + h) * DR * DC + (DR // 2 - rq) * DC + DC // 2 - (GRID_W - 1)
                        src = bass.AP(na_rpb.tensor, off, [[1, GRID_W], [DC, ROWS], [1, GRID_W]])
                        dst = braw[r0:r0 + GRID_W, h % 2, rq // 2, :].rearrange("p (r c) -> p r c", r=ROWS)
                        sp.dma_start(dst, src).then_inc(bias_in[h % 2], 16)

            for k, ph in enumerate(phases):
                nxt = following.get(k)
                for first, count, ada, last in sections(ph):
                    def body(i):
                        for par in range(2):
                            if not last:
                                load(ph, i + 1, par)
                            elif nxt:
                                load(nxt, 0, par)
                            if ada:
                                load_ada(ph, i, par)
                    iterate(sp, first, count, body)
                if ph.name == "v":
                    biases(ph.layer)
            for t in range(SEQ // P):
                sp.wait_ge(fin_ev, 2 * (t + 1))
                sp.dma_start(out[0, t * P:(t + 1) * P, :], fout[:, t, :]).then_inc(stored, 16)
            sp.wait_ge(stored, 16 * (SEQ // P))

        @block.gpsimd
        def _(pool):
            links = [0]

            def link(ins):
                links[0] += 1
                ins.then_inc(pool_c, 1)
                pool.wait_ge(pool_c, links[0])

            link(nc.gpsimd.memset(ident[:, :], 0.0))
            nc.gpsimd.affine_select(out=ident[:, :], in_=ident[:, :], compare_op=ALU.not_equal, fill=1.0,
                                    base=0, pattern=[[-1, P]], channel_multiplier=1).then_inc(consts, 1)
            nc.gpsimd.memset(ones[:, :], 1.0).then_inc(consts, 1)
            nc.gpsimd.memset(epst[:, :], EPS).then_inc(consts, 1)
            pool.wait_ge(consts, 3)
            link(nc.gpsimd.memset(flip[:, :], 0.0))
            for p0 in range(0, P, GRID_W):
                m = flip[p0:p0 + GRID_W, :]
                ins = nc.gpsimd.affine_select(out=m, in_=m, compare_op=ALU.not_equal, fill=1.0,
                                              base=-(p0 + GRID_W - 1), pattern=[[1, P]], channel_multiplier=1)
                ins.then_inc(consts, 1)
                pool.wait_ge(consts, 4 + p0 // GRID_W)
            link(nc.gpsimd.memset(mask[:, :], 0.0))
            hw = WIN_W // 2
            for p0 in range(0, P, GRID_W):
                m = mask[p0:p0 + GRID_W, 0:GRID_W - WIN_W]
                link(nc.gpsimd.affine_select(out=m, in_=m, compare_op=ALU.is_ge, fill=-BIG,
                                             base=hw - (GRID_W - 1), pattern=[[1, GRID_W - WIN_W]],
                                             channel_multiplier=1))
                m = mask[p0:p0 + GRID_W, WIN_W:GRID_W]
                link(nc.gpsimd.affine_select(out=m, in_=m, compare_op=ALU.is_ge, fill=-BIG,
                                             base=GRID_W - 1 + hw - 1 - WIN_W,
                                             pattern=[[-1, GRID_W - WIN_W]], channel_multiplier=-1))
            for g, win in enumerate(POOL_WINDOWS):
                hw = win // 2
                for e in range(hw):
                    nc.gpsimd.memset(ratio[:, g, e:e + 1], win / (e + hw))
                for e in range(1, hw):
                    nc.gpsimd.memset(ratio[:, g, 2 * PAD - e:2 * PAD - e + 1], win / (e + hw))
            wide_mask = mask[:, :].unsqueeze(1).to_broadcast([P, 2 * ROWS, GRID_W])

            def widest_sums():
                r = [q for q in range(2 * DEPTH) if pools(q)][0]
                pool.wait_ge(hh_done, KT * stream_base(r + 1))
                pool.wait_ge(pads_ready, 1)
                window_sums(len(POOL_WINDOWS) - 1, nc.gpsimd, link).then_inc(sums_ready, 1)

            for a, layer in enumerate(ATT):
                J, B = JOBS[layer], JBASE[layer]

                def masks(j, start):
                    for par in range(2):
                        pool.wait_ge(bias_in[par], (j + (a * KT + 1)) * 16 * ROWS)
                        if not start:
                            pool.wait_ge(nm_done, j * J + (B - J + par * (J // 2) + 2))
                        elif a:
                            pool.wait_ge(nm_done, B)
                        nc.gpsimd.tensor_tensor(
                            biasm[:, par, :, :].rearrange("p q (r c) -> p (q r) c", c=GRID_W),
                            braw[:, par, :, :].rearrange("p q (r c) -> p (q r) c", c=GRID_W),
                            wide_mask, ALU.add).then_inc(bias_ready, 1)
                masks(0, True)
                with pool.Fori(1, KT) as j:
                    masks(j, False)
                if a == 0:
                    widest_sums()

        @block.tensor
        def _(pe):
            mm, tp = nc.tensor.matmul, nc.tensor.transpose

            def reduce_ada(ph, i):
                a = i * 2 + (ph.ada_unit0 + 1)
                pe.wait_ge(ada_ops, a * 8 + 8)
                reduce_acc((i + ph.ada_group) * AG).then_inc(ada_reduced, 1)

            def reduce_acc(col):
                for s in range(2):
                    for t in range(AG):
                        ins = mm(adap[:, bass.ds(col + (s * NC + t), 1)], acc[:, s, t * P:(t + 1) * P],
                                 ones[:, 0:1], start=True, stop=True)
                return ins

            def source(ph, kt, par, n):
                if ph.name == "down":
                    t = par * ph.slabs + kt
                    return uhi[:, t, n], ulo[:, t, n]
                if ph.name == "scout":
                    return yhi[:, kt, n], ylo[:, kt, n]
                return hhi[:, kt, n], hlo[:, kt, n]

            def slab_wait(ph, i, par, kt):
                if ph.name == "scout" and par == 0 and kt % 2 == 0:
                    pe.wait_ge(u_done, ph.chunk0 - KT // 2 + kt // 2 + 1)
                elif ph.name == "down" and (par * ph.slabs + kt) % 2 == 0 or ph.name == "down" and kt == 0:
                    chunks = (HALF if ph.tile0 == 0 else FT - HALF) // 2
                    pe.wait_ge(u_done, ph.chunk0 - chunks + (par * ph.slabs + kt) // 2 + 1)

            def ready(ph, i, par):
                n = i * 2 + (ph.unit0 + par)
                if ph.name == "pool":
                    pe.wait_ge(u_done, ph.chunk0 + 2 * i + par + 1)
                pe.wait_ge(lo_done, n + 1)
                if not (isinstance(i, int) and n < 2):
                    pe.wait_ge(drained[par], i + ph.unit0 // 2)

            def slab(ph, i, par, kt, n):
                for m in range(2):
                    ins = products(ph, i, par, kt, n, m, pair[par][:, m, n])
                return ins

            def products(ph, i, par, kt, n, m, o):
                k0 = 2 * (2 * i + par) if ph.name == "pool" else 0
                a, b = source(ph, k0 + kt, par, n)
                w = slice(m * P, (m + 1) * P)
                mm(o, whi[:, par, kt, w], a, start=kt == 0, stop=False)
                mm(o, whi[:, par, kt, w], b, start=False, stop=False)
                return mm(o, wlo[:, par, kt, w], a, start=False, stop=kt == ph.slabs - 1)

            def first_units(ph):
                r = 2 * ph.layer + (1 if ph.name == "up" else 0)
                for s in range(ph.tokens // SEQ):
                    for par in range(2):
                        if s == 0:
                            ready(ph, 0, par)
                        for kt in range(ph.slabs):
                            if par == 0:
                                pe.wait_ge(h_done, h_base(r) + s * KT + kt + 1)
                            ins = slab(ph, 0, par, kt, cols(s))
                        if s == ph.tokens // SEQ - 1:
                            ins.then_inc(pe_done, 1)

            def last_unit(ph, i):
                ready(ph, i, 1)
                for s in range(2):
                    for q in range(2 * ph.slabs):
                        m, kt = q // ph.slabs, q % ph.slabs
                        ins = products(ph, i, 1, kt, cols(s), m, pair[1][:, s, cols(m)])
                        if s == 1 and q == min(2 * ph.slabs - 2, 8):
                            sum_squares(norm_of(ph), 0)
                    ins.then_inc(pe_done if s else half_done, 1)
                keep_warm(9)
                sum_squares(norm_of(ph), 1)

            def unit(ph, i, par, start, reduced=None):
                ready(ph, i, par)
                out = pair[par]
                if ph.name == "v":
                    for tt in range(ph.tokens // P):
                        t = slice(tt * P, (tt + 1) * P)
                        o = out[:, tt // 2, tt % 2 * UC:(tt % 2 + 1) * UC]
                        for kt in range(ph.slabs):
                            mm(o, hhi[:, kt, t], whi[:, par, kt, :], start=kt == 0, stop=False)
                            mm(o, hlo[:, kt, t], whi[:, par, kt, :], start=False, stop=False)
                            ins = mm(o, hhi[:, kt, t], wlo[:, par, kt, :], start=False,
                                     stop=kt == ph.slabs - 1)
                        if reduced and tt == 0:
                            reduce_ada(*reduced)
                    ins.then_inc(pe_done, 1)
                    return
                for kt in range(ph.slabs):
                    if start:
                        slab_wait(ph, i, par, kt)
                    ins = slab(ph, i, par, kt, slice(0, ph.tokens))
                    if reduced and kt == ph.slabs // 2:
                        reduce_ada(*reduced)
                ins.then_inc(pe_done, 1)

            def keep_warm(count):
                for _ in range(count):
                    mm(ptb[1][:, 0:P], ident[:, :], ident[:, :], start=True, stop=True)

            def sum_squares(r, s):
                pe.wait_ge(acc_done, 7 * (r + 1))
                mm(ssb[s], ones[:, :], acc2[:, 0, cols(s)], start=True, stop=False)
                mm(ssb[s], ones[:, :], acc2[:, 1, cols(s)], start=False, stop=False)
                pe.wait_ge(sq_done, KT * r + (KT - 1 + s if streams(r) == 2 else KT))
                for m in range(2):
                    ins = mm(ssb[s], ones[:, :], sq[:, m, cols(s)], start=False, stop=m == 1)
                ins.then_inc(ss_done, 1)

            def attention(layer):
                J, B = JOBS[layer], JBASE[layer]
                NJ = J * KT
                last_v = [p for p in phases if p.name == "v" and p.layer == layer][0]
                uses = (last_v.unit0 + last_v.units) // 2
                keep_warm(6)
                pe.wait_ge(drained[0], uses)
                pe.wait_ge(drained[1], uses)

                def scores(t):
                    p, qt = job(layer, t % J)
                    j, f = t // J, slice(HD * p, HD * (p + 1))
                    w = width(qt)
                    if t >= 4:
                        pe.wait_ge(p_done, B + t - 3)
                    mm(sbank[t % 4][:, TOK - w:TOK], qT[f, j, qt * P:(qt + 1) * P], kT[f, j, TOK - w:TOK],
                       start=True, stop=True).then_inc(s_done, 1)

                def turn(t):
                    _, qt = job(layer, t % J)
                    pe.wait_ge(p_done, B + t + 1)
                    if t >= 2:
                        pe.wait_ge(pt_done, B + t - 1)
                    for k in range(width(qt) // P):
                        ins = tp(ptb[t % 2][:, k * P:(k + 1) * P], prob[:, t % 4, k * P:(k + 1) * P],
                                 ident[:, :])
                    ins.then_inc(tr_done, 1)

                def values(t):
                    p, qt = job(layer, t % J)
                    j = t // J
                    n = width(qt) // P
                    pe.wait_ge(pt_done, B + t + 1)
                    if t >= 2:
                        pe.wait_ge(o_done, B + t - 1)
                    if j >= 1 and t % J < 2:
                        pe.wait_ge(ot_free, 2 * (KT * ATT.index(layer) + j) - 1 + t % J)
                    c0 = (2 * j + p) * HD
                    for k in range(n):
                        ins = mm(obank[t % 2][:, 0:HD], ptsb[:, t % 2, k * P:(k + 1) * P],
                                 vt[:, TOK // P - n + k, c0:c0 + HD], start=k == 0, stop=k == n - 1)
                    ins.then_inc(pv_done, 1)

                def turn_out(j):
                    pe.wait_ge(o_done, B + J * (j + 1))
                    n = J // 4
                    for half in range(2):
                        for k in range(n):
                            ins = mm(obank[half][:, k * P:(k + 1) * P], otok[:, half * n + k, :], flip[:, :],
                                     start=True, stop=True)
                        ins.then_inc(ot_done, 1)

                scores(0)
                scores(1)
                scores(2)
                keep_warm(8)
                for t in range(NJ + 1):
                    if t + 3 < NJ:
                        scores(t + 3)
                    if t < NJ:
                        turn(t)
                    if t % J == 1 and t > J:
                        turn_out(t // J - 1)
                    if t >= 1:
                        values(t - 1)
                turn_out(KT - 1)

            pe.wait_ge(consts, 5)
            pe.wait_ge(small_in, 16 * len(small_parts))
            for t in range(3):
                n = min(P, V_END - t * P)
                ins = tp(ptb[0][:, t * P:t * P + n], stage[0:n, t, :], ident[0:n, 0:n])
            ins.then_inc(vt_done, 1)

            def turn_x(kt):
                if kt >= 4:
                    pe.wait_ge(x_init, kt - 3)
                for tt in range(TOK // P):
                    ins = tp(sbank[kt % 4][:, tt * P:(tt + 1) * P], xtok[:, tt, kt * P:(kt + 1) * P],
                             ident[:, :])
                ins.then_inc(xtr_done, 1)

            def first_ada(q):
                pe.wait_ge(apro_in[PE_GROUPS[q]], 16)
                if q >= 2:
                    pe.wait_ge(arow_done, q - 1)
                for kt in range(KT):
                    ins = mm(ptb[q % 2][0:2, :], sc[:, kt, :], apro[PE_GROUPS[q]][:, kt, :], start=kt == 0,
                             stop=kt == KT - 1)
                ins.then_inc(apro_done, 1)

            def turn_ada(q):
                pe.wait_ge(arow_done, q + 1)
                for t in range(AG):
                    col = PE_GROUPS[q] * AG + t
                    ins = tp(adap[:, col:col + NC + 1:NC], arow[0:2, q % 2, t * P:(t + 1) * P], ident[0:2, 0:2])
                ins.then_inc(arow_out, 1)

            pe.wait_ge(x_in[0], 16)
            pe.wait_ge(x_in[1], 16)
            for kt in range(KT):
                turn_x(kt)
            pe.wait_ge(silu_done, 1)
            first_ada(0)
            sum_squares(0, 0)
            sum_squares(0, 1)
            first_ada(1)
            pe.wait_ge(sd_done, 2)
            turn_ada(0)
            pe.wait_ge(pro_ops, 2 * KT)
            reduce_acc(DVE_GROUP * AG).then_inc(arow_out, 1)
            first_ada(2)
            turn_ada(1)
            turn_ada(2)

            owed = None
            for ph in phases:
                if ph.name == "wo":
                    pe.wait_ge(ot_free, 2 * KT * (ATT.index(ph.layer) + 1))
                total = ph.units // 2
                cuts = sorted({0, 1, ph.ada_from + 1, min(ph.ada_to + 1, total), total - 1, total})
                for first, end in zip(cuts, cuts[1:]):
                    def body(i):
                        if first == 0:
                            reduced = owed
                        else:
                            reduced = (ph, i - 1) if ph.ada_from < first <= ph.ada_to else None
                        if ph.fresh and first == 0:
                            first_units(ph)
                            if reduced:
                                reduce_ada(*reduced)
                            return
                        unit(ph, i, 0, first == 0, reduced)
                        if finals(ph) and streams(norm_of(ph)) == 2 and end == total and end - first == 1:
                            last_unit(ph, i)
                        else:
                            unit(ph, i, 1, first == 0)
                    iterate(pe, first, end - first, body)
                owed = (ph, total - 1) if ph.ada_to == total else None
                if owed and ph.name == "v":
                    reduce_ada(*owed)
                    owed = None
                if ph.name == "v":
                    attention(ph.layer)
                if finals(ph):
                    if streams(norm_of(ph)) == 1:
                        sum_squares(norm_of(ph), 0)
                        if norm_of(ph) < 2 * DEPTH:
                            keep_warm(12)
            for t in range(SEQ // P):
                for kt in range(KT):
                    if t == 0:
                        pe.wait_ge(t_done, KT * stream_base(2 * DEPTH) + kt + 1)
                    ins = tp(sbank[2 * t + kt // 4][:, kt % 4 * P:(kt % 4 + 1) * P],
                             fin[:, kt, t * P:(t + 1) * P], ident[:, :])
                ins.then_inc(fin_tr, 1)

        @block.scalar
        def _(act):
            go = nc.scalar.activation

            def split_hi(ph, i, par):
                n = i * 2 + (ph.unit0 + par)
                act.wait_ge(raw_in[par], (i + (ph.unit0 // 2 + 1)) * 16)
                if not (isinstance(i, int) and n < 2):
                    act.wait_ge(pe_done, n - 1)
                go(whi[:, par, 0:ph.slabs, :], raw[:, par, 0:ph.slabs, :], ACT.Copy).then_inc(hi_done, 1)

            def square(r, i, m, n):
                if not (isinstance(i, int) and i == 0):
                    act.wait_ge(acc_done, i * 2 + (7 * r + m))
                elif r:
                    act.wait_ge(ss_done, stream_base(r))
                go(sq[:, m, 0:n], xT[:, i * 2 + m, 0:n], ACT.Square).then_inc(sq_done, 1)

            def last_squares(r, s):
                act.wait_ge(acc_done, 7 * (r + 1))
                for m in range(2):
                    ins = go(sq[:, m, cols(s)], xT[:, KT - 2 + m, cols(s)], ACT.Square)
                    if m or streams(r) == 1:
                        ins.then_inc(sq_done, 1)

            def drain(ph, i, par):
                n = ph.tokens
                u = i * 2 + par
                nn = i * 2 + (ph.unit0 + par)
                src = pair[par][:, :, 0:n]
                if ph.name in ("q", "k"):
                    act.wait_ge(pe_done, nn + 1)
                    if ph.name == "k":
                        go(kT[:, bass.ds(u * 2, 2), 0:n], src, ACT.Copy).then_inc(drained[par], 1)
                        return
                    for m in range(2):
                        first = pair[par][:, m, GRID_W - 1:GRID_W]
                        turned = bass.AP(first.tensor, first.offset,
                                         [list(first.ap[0]), [GRID_W, n // GRID_W], [-1, GRID_W]])
                        ins = go(qT[:, u * 2 + m, 0:n].rearrange("p (r c) -> p r c", c=GRID_W), turned,
                                 ACT.Copy, scale=SCALE)
                    ins.then_inc(drained[par], 1)
                elif ph.name == "v":
                    act.wait_ge(pe_done, nn + 1)
                    go(vt[:, :, bass.ds(u * UC, UC)],
                       pair[par][:, :, :].rearrange("p a (b c) -> p (a b) c", c=UC), ACT.Copy)\
                        .then_inc(drained[par], 1)
                elif ph.name == "up" and par == 0:
                    act.wait_ge(pe_done, nn + 1)
                    act.wait_ge(drained[1], i + ph.unit0 // 2)
                    go(gs[:, :, 0:n], src, ACT.Silu).then_inc(drained[par], 1)
                elif ph.name == "conv" and par == 0:
                    act.wait_ge(pe_done, nn + 1)
                    act.wait_ge(drained[1], i + ph.unit0 // 2)
                    go(gs[:, :, 0:n], src, ACT.Copy).then_inc(drained[par], 1)

            def chunk_hi(dst, n, ready, count):
                act.wait_ge(ready, count)
                go(dst, tb[:, :, 0:n], ACT.Copy).then_inc(uhi_done, 1)

            def pool_hi(g):
                chunk_hi(hhi[:, 2 * g:2 * g + 2, :], TOK, tb_ready, g + 1)

            def root(r, s):
                act.wait_ge(ss_done, stream_base(r) + s + 1)
                if r and s == 0:
                    act.wait_ge(t_done, KT * stream_base(r))
                go(rstd[:, cols(s)], ssb[s], ACT.Sqrt, bias=epst[:, 0:1], scale=1.0 / D)\
                    .then_inc(sd_done, 1)

            def norm(r):
                layer, mix = r // 2, r % 2 == 0
                if r == 2 * DEPTH:
                    return
                for s in range(streams(r)):
                    for kt in range(KT):
                        p = s * KT + kt
                        act.wait_ge(t_done, KT * stream_base(r) + p + 1)
                        b0 = (0 if mix else 3) * KT + kt
                        dst = hp[:, 2 * kt + s, PAD:PAD + SEQ] if pools(r) else hhi[:, kt, cols(s)]
                        go(dst, tr[:, p % TR, :], ACT.Identity, bias=modv[:, layer % 2, s, b0:b0 + 1])\
                            .then_inc(hh_done, 1)
                        if p == 1 and r and streams(r) == 2:
                            root(r, 1)
            def attention(layer):
                J, B = JOBS[layer], JBASE[layer]
                a = ATT.index(layer)

                def exps(j, idx, start):
                    _, qt = job(layer, idx)
                    w = width(qt)
                    t = j * J + (B + idx)
                    act.wait_ge(nm_done, t + 1)
                    if not (start and idx < 4):
                        act.wait_ge(tr_done, t - 3)
                    if not start:
                        act.wait_ge(o_done, t - J + 1)
                    go(prob[:, idx % 4, 0:w], sbank[idx % 4][:, TOK - w:TOK], ACT.Exp,
                       bias=nmx[:, idx:idx + 1], accum_out=rsum[:, idx:idx + 1]).then_inc(p_done, 1)

                def copy_turned(j, idx, start):
                    _, qt = job(layer, idx)
                    t = j * J + (B + idx)
                    act.wait_ge(tr_done, t + 1)
                    if not (start and idx < 2):
                        act.wait_ge(pv_done, t - 1)
                    go(ptsb[:, idx % 2, 0:width(qt)], ptb[idx % 2][:, 0:width(qt)], ACT.Copy)\
                        .then_inc(pt_done, 1)

                def out_hi(j):
                    n = J // 4 * P
                    for half in range(2):
                        act.wait_ge(ot_done, j * 2 + (2 * KT * a + half + 1))
                        go(hhi[:, j, half * n:(half + 1) * n], obank[half][:, 0:n], ACT.Copy)\
                            .then_inc(ot_hi, 1)

                def tile(j, start):
                    for idx in range(J):
                        exps(j, idx, start)
                        if idx:
                            copy_turned(j, idx - 1, start)
                        elif not start:
                            copy_turned(j - 1, J - 1, False)
                        if idx == 1 and not start:
                            out_hi(j - 1)

                tile(0, True)
                with act.Fori(1, KT) as j:
                    tile(j, False)
                copy_turned(KT - 1, J - 1, False)
                out_hi(KT - 1)

            for src, t, r0, n in small_parts:
                act.dma_start(stage[r0:r0 + n, t, :], src).then_inc(small_in, 16)
            act.wait_ge(vt_done, 1)
            go(vecs[:, 0:V_END], ptb[0][:, 0:V_END], ACT.Copy).then_inc(vecs_done, 1)
            act.wait_ge(vecs_done, 1)
            go(sc[:, :, :], vecs[:, V_C:V_END].rearrange("p (s k) -> p k s", s=2), ACT.Silu)\
                .then_inc(silu_done, 1)

            def copy_rows(q):
                act.wait_ge(apro_done, q + 1)
                if q >= 2:
                    act.wait_ge(arow_out, q - 1)
                go(arow[0:2, q % 2, :], ptb[q % 2][0:2, :], ACT.Copy).then_inc(arow_done, 1)

            for kt in range(KT):
                act.wait_ge(x_init, kt + 1)
                if kt < KT - 2:
                    square(0, kt // 2, kt % 2, TOK)
            for s in range(2):
                last_squares(0, s)
            copy_rows(0)
            root(0, 0)
            root(0, 1)
            copy_rows(1)
            split_hi(phases[0], 0, 0)
            split_hi(phases[0], 0, 1)
            copy_rows(2)
            norm(0)

            for k, ph in enumerate(phases):
                nxt = following.get(k)
                if finals(ph) or ph.name == "v":
                    go(preload[:, k:k + 1], epst[:, 0:1], ACT.Exp if ph.name == "v" else ACT.Sqrt)
                for first, count, ada, last in sections(ph):
                    def body(i):
                        for par in range(2):
                            drain(ph, i, par)
                            if not last:
                                split_hi(ph, i + 1, par)
                            elif nxt and not (finals(ph) and par == 1):
                                split_hi(nxt, 0, par)
                            if ph.name == "pool" and not last:
                                pool_hi(i * 2 + par + 2)
                            if ph.name == "up" and par == 1:
                                chunk_hi(uhi[:, bass.ds(i * 2, 2), 0:ph.tokens], ph.tokens,
                                         drained[1], i + (ph.unit0 // 2 + 1))
                            if ph.name == "gateb":
                                chunk_hi(yhi[:, bass.ds((i * 2 + par) * 2, 2), 0:ph.tokens], ph.tokens,
                                         drained[par], i + (ph.unit0 // 2 + 1))
                            if finals(ph):
                                if last and par == 1:
                                    continue
                                elif ph.name != "down":
                                    q = i * 2 + par
                                elif par == 1:
                                    q = i
                                else:
                                    continue
                                r = norm_of(ph)
                                act.wait_ge(xt_done, q + pair_base(r) + 1)
                                square(r, q, 0, ph.tokens)
                                act.wait_ge(drained[par], i + (ph.unit0 // 2 + 1))
                                square(r, q, 1, ph.tokens)
                    iterate(act, first, count, body)
                if ph.name == "v":
                    attention(ph.layer)
                if finals(ph):
                    r = norm_of(ph)
                    for s in range(streams(r)):
                        if s == 0 and streams(r) == 2:
                            act.wait_ge(xt_done, pair_base(r + 1))
                        else:
                            act.wait_ge(drained[1], (ph.unit0 + ph.units) // 2)
                        last_squares(r, s)
                        if s == 0:
                            root(r, 0)
                            if nxt:
                                split_hi(nxt, 0, 1)
                    norm(r)
                    if pools(r):
                        for g in range(2):
                            pool_hi(g)
            for t in range(SEQ // P):
                act.wait_ge(fin_tr, t + 1)
                for b in range(2):
                    go(fout[:, t, b * 512:(b + 1) * 512], sbank[2 * t + b], ACT.Copy).then_inc(fin_ev, 1)

        @block.vector
        def _(dve):
            links = [0]

            def link(ins):
                links[0] += 1
                ins.then_inc(chain_s, 1)
                dve.wait_ge(chain_s, links[0])

            tt, ts, stt = nc.vector.tensor_tensor, nc.vector.tensor_scalar, nc.vector.scalar_tensor_tensor

            def split_lo(ph, i, par):
                n = i * 2 + (ph.unit0 + par)
                dve.wait_ge(hi_done, n + 1)
                tt(wlo[:, par, 0:ph.slabs, :], raw[:, par, 0:ph.slabs, :],
                   whi[:, par, 0:ph.slabs, :].bitcast(F32), ALU.subtract).then_inc(lo_done, 1)

            def ada(ph, i, par):
                a = i * 2 + (ph.ada_unit0 + par)
                dve.wait_ge(ada_in[par], (i + (ph.ada_unit0 // 2 + 1)) * 16)
                if par == 0 and not (isinstance(i, int) and a < 2):
                    dve.wait_ge(ada_reduced, i + ph.ada_unit0 // 2)
                for k in range(4):
                    for s in range(2):
                        o = 2 * k + s
                        src = araw[:, par, k, :]
                        w = sc[:, 4 * par + k, s:s + 1]
                        if par == 0 and k == 0:
                            ins = ts(acc[:, s, :], src, w, None, ALU.mult)
                        else:
                            dve.wait_ge(ada_ops, a * 8 + (o - 1))
                            ins = stt(out=acc[:, s, :], in0=src, scalar=w, in1=acc[:, s, :],
                                      op0=ALU.mult, op1=ALU.add)
                        ins.then_inc(ada_ops, 1)

            def take_mod(layer, part0, part1, extra=None):
                c0, c1 = part0 * KT, part1 * KT
                for s in range(2):
                    ins = tt(modv[:, layer % 2, s, c0:c1], adap[:, s * NC + c0:s * NC + c1],
                             vecs[:, V_B + layer * NC + c0:V_B + layer * NC + c1], ALU.add)
                link(ins)

            def chunk_lo(chunk, hi, lo, n):
                dve.wait_ge(uhi_done, chunk + 1)
                tt(lo, tb[:, :, 0:n], hi.bitcast(F32), ALU.subtract).then_inc(u_done, 1)

            def residual(ph, i, par, q, last_sum):
                part = 5 if ph.name == "down" else 2
                for m in range(2):
                    for s in range(ph.tokens // SEQ):
                        xa = xT[:, q * 2 + m, cols(s)]
                        if ph.name == "pool":
                            gate = pgate[:, s, bass.ds(q * 2 + m, 1)]
                        else:
                            gate = modv[:, ph.layer % 2, s, bass.ds(q * 2 + (part * KT + m), 1)]
                        ins = stt(out=xa, in0=pair[par][:, m, cols(s)], scalar=gate, in1=xa,
                                  op0=ALU.mult, op1=ALU.add)
                    if last_sum and m == 0:
                        ins.then_inc(xt_done, 1)
                ins.then_inc(drained[par], 1)

            def last_residual(ph, s):
                part = 5 if ph.name == "down" else 2
                if ph.name == "down":
                    dve.wait_ge(drained[0], (ph.unit0 + ph.units) // 2)
                if s == 0:
                    dve.wait_ge(half_done, norm_of(ph))
                else:
                    dve.wait_ge(pe_done, ph.unit0 + ph.units)
                for m in range(2):
                    t = KT - 2 + m
                    c0 = part * KT + t
                    gate = pgate[:, s, t:t + 1] if ph.name == "pool" else modv[:, ph.layer % 2, s, c0:c0 + 1]
                    ins = stt(out=xT[:, t, cols(s)], in0=pair[1][:, s, cols(m)], scalar=gate,
                              in1=xT[:, t, cols(s)], op0=ALU.mult, op1=ALU.add)
                ins.then_inc(drained[1] if s else xt_done, 1)

            def add_squares(r, q, n):
                for m in range(2):
                    dve.wait_ge(sq_done, q * 2 + (KT * r + m + 1))
                    dve.wait_ge(acc_done, q * 2 + (7 * r + m + 1))
                    tt(acc2[:, m, 0:n], acc2[:, m, 0:n], sq[:, m, 0:n], ALU.add).then_inc(acc_done, 1)

            def start_squares(r):
                if r:
                    dve.wait_ge(ss_done, stream_base(r))
                nc.vector.memset(acc2[:, :, :], 0.0).then_inc(acc_done, 1)

            def scales(r):
                if r == 2 * DEPTH:
                    return
                layer, mix = r // 2, r % 2 == 0
                v0 = (V_GM if mix else V_GF) + layer * KT
                p0 = (1 if mix else 4) * KT
                for s in range(streams(r)):
                    ins = stt(out=moda[:, s, :], in0=modv[:, layer % 2, s, p0:p0 + KT], scalar=1.0,
                              in1=vecs[:, v0:v0 + KT], op0=ALU.add, op1=ALU.mult)
                link(ins)

            def reciprocal(r, s):
                dve.wait_ge(sd_done, stream_base(r) + s + 1)
                link(nc.vector.reciprocal(rstd[:, cols(s)], rstd[:, cols(s)]))

            def norm(r, nxt):
                layer, mix = r // 2, r % 2 == 0
                base = KT * stream_base(r)
                pieces = KT * streams(r)

                def scaled(p):
                    s, kt = p // KT, p % KT
                    if p >= TR and r < 2 * DEPTH:
                        if pools(r):
                            dve.wait_ge(hh_done, base + p - TR + 1)
                        else:
                            dve.wait_ge(h_done, h_base(r) + p - TR + 1)
                    final = r == 2 * DEPTH
                    stt(out=fin[:, kt, :] if final else tr[:, p % TR, :], in0=xT[:, kt, cols(s)],
                        scalar=vecs[:, V_FG + kt:V_FG + kt + 1] if final else moda[:, s, kt:kt + 1],
                        in1=rstd[:, cols(s)], op0=ALU.mult, op1=ALU.mult).then_inc(t_done, 1)

                def low(p):
                    s, kt = p // KT, p % KT
                    dve.wait_ge(hh_done, base + p + 1)
                    c0 = (0 if mix else 3) * KT + kt
                    stt(out=hlo[:, kt, cols(s)], in0=tr[:, p % TR, :],
                        scalar=modv[:, layer % 2, s, c0:c0 + 1],
                        in1=hhi[:, kt, cols(s)].bitcast(F32), op0=ALU.add, op1=ALU.subtract)\
                        .then_inc(h_done, 1)

                for p in range(pieces + 1):
                    if p < pieces and p != KT:
                        scaled(p)
                    if p and r < 2 * DEPTH and not pools(r):
                        low(p - 1)
                    if p == KT and nxt:
                        split_lo(nxt, 0, 1)
                    if p == KT and streams(r) == 2:
                        reciprocal(r, 1)
                        scaled(p)
                if pools(r):
                    dve.wait_ge(hh_done, base + pieces)

            def pooled_tiles(ph, g):
                win = POOL_WINDOWS[g]
                hw = win // 2
                if g == len(POOL_WINDOWS) - 1:
                    dve.wait_ge(sums_ready, 1)
                else:
                    link(window_sums(g, nc.vector, link))
                sums = pw[:, 2 if g == len(POOL_WINDOWS) - 1 else g % 2, g % 2, :, PAD:PAD + SEQ]
                for c0, n in ((0, hw), (SEQ - hw + 1, hw - 1)):
                    if n:
                        e0 = 0 if c0 == 0 else 2 * PAD - n
                        ins = tt(sums[:, :, c0:c0 + n], sums[:, :, c0:c0 + n],
                                 ratio[:, g, e0:e0 + n].unsqueeze(1).to_broadcast([P, 4, n]), ALU.mult)
                link(ins)
                dve.wait_ge(u_done, ph.chunk0 + g)
                stt(out=tb[:, :, :].rearrange("p m (s t) -> p (m s) t", s=2), in0=sums, scalar=1.0 / win,
                    in1=hp[:, 4 * g:4 * g + 4, PAD:PAD + SEQ], op0=ALU.mult, op1=ALU.subtract)\
                    .then_inc(tb_ready, 1)
                chunk_lo(ph.chunk0 + g, hhi[:, 2 * g:2 * g + 2, :], hlo[:, 2 * g:2 * g + 2, :], TOK)

            def attention(layer):
                J, B = JOBS[layer], JBASE[layer]
                a = ATT.index(layer)

                def maxima(j, idx):
                    p, qt = job(layer, idx)
                    t = j * J + (B + idx)
                    s = sbank[idx % 4]
                    dve.wait_ge(s_done, t + 1)
                    if width(qt) == TOK:
                        dve.wait_ge(bias_ready, j * 2 + (a * HEADS + p + 1))
                    ins = nc.vector.reduce_max(mx[:, 1, idx:idx + 1], s[:, SEQ:TOK], AXX)
                    if width(qt) == TOK:
                        ins = nc.vector.tensor_tensor_reduce(s[:, 0:SEQ], s[:, 0:SEQ], biasm[:, p, qt, :], 1.0,
                                                             -BIG, ALU.add, ALU.max, mx[:, 0, idx:idx + 1])
                    ins.then_inc(mx_done, 1)
                    dve.wait_ge(mx_done, t + 1)
                    if width(qt) == TOK:
                        ins = ts(nmx[:, idx:idx + 1], mx[:, 0, idx:idx + 1], mx[:, 1, idx:idx + 1], -1.0,
                                 ALU.max, ALU.mult)
                    else:
                        ins = ts(nmx[:, idx:idx + 1], mx[:, 1, idx:idx + 1], -1.0, None, ALU.mult)
                    ins.then_inc(nm_done, 1)

                def normalise(j, idx, start):
                    p, qt = job(layer, idx)
                    t = j * J + (B + idx)
                    dve.wait_ge(pv_done, t + 1)
                    nc.vector.reciprocal(rinv[:, idx:idx + 1], rsum[:, idx:idx + 1]).then_inc(ri_done, 1)
                    dve.wait_ge(ri_done, t + 1)
                    if idx == 0 and not start:
                        dve.wait_ge(ot_done, j * 2 + 2 * KT * a)
                    ts(otok[:, qt, p * HD:(p + 1) * HD], obank[idx % 2][:, 0:HD], rinv[:, idx:idx + 1], None,
                       ALU.mult).then_inc(o_done, 1)

                def out_lo(j):
                    n = J // 4 * P
                    for half in range(2):
                        dve.wait_ge(ot_hi, j * 2 + (2 * KT * a + half + 1))
                        c0 = half * n
                        tt(hlo[:, j, c0:c0 + n], obank[half][:, 0:n], hhi[:, j, c0:c0 + n].bitcast(F32),
                           ALU.subtract).then_inc(ot_free, 1)

                def tile(j, start):
                    for idx in range(J):
                        maxima(j, idx)
                        if idx == 3 and not start:
                            out_lo(j - 1)
                        if idx >= 3:
                            normalise(j, idx - 3, start)
                        elif not start:
                            normalise(j - 1, J - 3 + idx, False)

                tile(0, True)
                with dve.Fori(1, KT) as j:
                    tile(j, False)
                normalise(KT - 1, J - 3, False)
                normalise(KT - 1, J - 2, False)
                normalise(KT - 1, J - 1, False)
                out_lo(KT - 1)

            def drain(ph, i, par):
                n = ph.tokens
                nn = i * 2 + (ph.unit0 + par)
                if ph.name == "up" and par == 1:
                    dve.wait_ge(drained[0], i + (ph.unit0 // 2 + 1))
                    if not (isinstance(i, int) and i + ph.chunk0 == 0):
                        dve.wait_ge(u_done, i + ph.chunk0)
                    dve.wait_ge(pe_done, nn + 1)
                    tt(tb[:, :, 0:n], gs[:, :, 0:n], pair[1][:, :, 0:n], ALU.mult).then_inc(drained[1], 1)
                elif ph.name == "gateb":
                    dve.wait_ge(conv_ops, 6 * KT // 2)
                    dve.wait_ge(u_done, i * 2 + (ph.chunk0 + par))
                    dve.wait_ge(pe_done, nn + 1)
                    tt(tb[:, :, 0:n], cv[:, bass.ds((i * 2 + par) * 2, 2), 0:n], pair[par][:, :, 0:n], ALU.mult)\
                        .then_inc(drained[par], 1)
                elif ph.name == "conv" and par == 1:
                    dve.wait_ge(drained[0], i + (ph.unit0 // 2 + 1))
                    dve.wait_ge(pe_done, nn + 1)
                    if not (isinstance(i, int) and i == 0):
                        dve.wait_ge(conv_ops, i * 6)
                    tt(tb[:, :, 0:n], gs[:, :, 0:n], pair[1][:, :, 0:n], ALU.mult).then_inc(drained[1], 1)
                    dve.wait_ge(drained[1], i + (ph.unit0 // 2 + 1))
                    o = 0
                    for tap, (d0, s0) in ((1, (0, 0)), (0, (1, 0)), (2, (0, 1))):
                        w = SEQ - (tap != 1)
                        for m in range(2):
                            dst = cv[:, i * 2 + m, :].rearrange("p (s t) -> p s t", s=2)[:, :, d0:d0 + w]
                            src = tb[:, m, :].rearrange("p (s t) -> p s t", s=2)[:, :, s0:s0 + w]
                            wt = vecs[:, bass.ds(i * 2 + (V_CW + tap * KT + m), 1)]
                            if tap == 1:
                                ins = ts(dst, src, wt, None, ALU.mult)
                            else:
                                dve.wait_ge(conv_ops, i * 6 + (o - 1))
                                ins = stt(out=dst, in0=src, scalar=wt, in1=dst, op0=ALU.mult, op1=ALU.add)
                            ins.then_inc(conv_ops, 1)
                            o += 1
                elif ph.name in ("wo", "scout", "pool"):
                    dve.wait_ge(pe_done, nn + 1)
                    residual(ph, i, par, i * 2 + par, True)
                elif ph.name == "down":
                    dve.wait_ge(pe_done, nn + 1)
                    dve.wait_ge(drained[1 - par], i + (ph.unit0 // 2 + par))
                    residual(ph, i, par, i, par == 1 and finals(ph))

            start_squares(0)
            for kt in range(KT):
                dve.wait_ge(xtr_done, kt + 1)
                nc.vector.tensor_copy(xT[:, kt, :], sbank[kt % 4]).then_inc(x_init, 1)
                if kt % 2 and kt < KT - 1:
                    add_squares(0, kt // 2, TOK)
            dve.wait_ge(silu_done, 1)
            dve.wait_ge(apro_in[DVE_GROUP], 16)
            for o in range(2 * KT):
                k, st = o // 2, o % 2
                src, w = apro[DVE_GROUP][:, k, :], sc[:, k, st:st + 1]
                if k == 0:
                    ins = ts(acc[:, st, :], src, w, None, ALU.mult)
                else:
                    dve.wait_ge(pro_ops, o - 1)
                    ins = stt(out=acc[:, st, :], in0=src, scalar=w, in1=acc[:, st, :], op0=ALU.mult, op1=ALU.add)
                ins.then_inc(pro_ops, 1)
            reciprocal(0, 0)
            split_lo(phases[0], 0, 0)
            split_lo(phases[0], 0, 1)
            dve.wait_ge(vecs_done, 1)
            dve.wait_ge(arow_out, PG)
            take_mod(0, 0, 2)
            scales(0)
            norm(0, None)

            for k, ph in enumerate(phases):
                nxt = following.get(k)
                if finals(ph):
                    start_squares(norm_of(ph))
                split_last = finals(ph) and streams(norm_of(ph)) == 2
                for first, count, with_ada, last in sections(ph):
                    def body(i):
                        for par in range(2):
                            if with_ada and not (last and par == 1 and split_last):
                                ada(ph, i, par)
                            if last and par == 1 and split_last:
                                last_residual(ph, 0)
                                split_lo(nxt, 0, 0)
                                scales(norm_of(ph))
                                reciprocal(norm_of(ph), 0)
                                last_residual(ph, 1)
                            else:
                                drain(ph, i, par)
                            if ph.name == "gateb":
                                q = i * 2 + par
                                t = bass.ds(q * 2, 2)
                            if not last:
                                split_lo(ph, i + 1, par)
                            elif nxt and not (finals(ph) and par == 1) and not split_last:
                                split_lo(nxt, 0, par)
                            if ph.name == "pool" and not last:
                                pooled_tiles(ph, i * 2 + par + 2)
                            if ph.name == "up" and par == 1:
                                t = bass.ds(i * 2, 2)
                                chunk_lo(i + ph.chunk0, uhi[:, t, 0:ph.tokens], ulo[:, t, 0:ph.tokens], ph.tokens)
                            if ph.name == "gateb":
                                chunk_lo(q + ph.chunk0, yhi[:, t, :], ylo[:, t, :], ph.tokens)
                            if finals(ph):
                                if ph.name != "down":
                                    if not (last and par == 1):
                                        add_squares(norm_of(ph), i * 2 + par, ph.tokens)
                                elif par == 1 and not last:
                                    add_squares(norm_of(ph), i, ph.tokens)
                    if ph.name == "up" and ph.layer == 0 and not ph.tile0 and last:
                        dve.wait_ge(ada_reduced, ph.ada_unit0 // 2 + ph.ada_to - 1)
                        take_mod(0, 5, 6)
                    if ph.name == "down" and ph.tile0 and ph.layer < DEPTH - 1 and last:
                        dve.wait_ge(ada_reduced, ph.ada_unit0 // 2)
                        take_mod(ph.layer + 1, 0, N_MOD)
                    iterate(dve, first, count, body)
                if ph.name == "v":
                    if ph.ada_to:
                        dve.wait_ge(ada_reduced, ph.ada_unit0 // 2 + ph.ada_to)
                        take_mod(0, 2, 5)
                    attention(ph.layer)
                if finals(ph):
                    r = norm_of(ph)
                    pooled = pools(r)
                    if pooled:
                        nl = r // 2
                        for s in range(2):
                            ins = tt(pgate[:, s, :], modv[:, nl % 2, s, 2 * KT:3 * KT],
                                     vecs[:, V_PS:V_PS + KT], ALU.mult)
                        nc.vector.memset(hp[:, :, 0:PAD], 0.0)
                        nc.vector.memset(hp[:, :, PAD + SEQ:PW], 0.0).then_inc(pads_ready, 1)
                    if not split_last:
                        scales(r)
                        reciprocal(r, 0)
                    norm(r, nxt)
                    if ph.ada_to == ph.units // 2:
                        ada(ph, ph.ada_to - 1, 1)
                    if pooled:
                        pooled_tiles(following[k], 0)
                        pooled_tiles(following[k], 1)


_INS = ["x", "c", "ctx", "c_ctx", "adaln_w", "adaln_b", "norm_mix_g", "norm_ffn_g", "ffn_w1", "ffn_w3",
        "ffn_w2", "na_w_qkv", "na_w_o", "na_rpb", "sc_w_in", "sc_conv_w", "sc_w_out", "pool_w",
        "pool_scale", "final_g"]


def kernel(**inputs):
    import numpy as _np
    import concourse.bacc as _bacc
    from concourse import mybir as _mybir
    from concourse.bass_utils import run_bass_kernel_spmd as _run

    nc = _bacc.Bacc("TRN2", target_bir_lowering=False, num_devices=1)
    arrays, args = {}, []
    for name in _INS:
        a = _np.ascontiguousarray(inputs[name])
        arrays[f"in_{name}_dram"] = a
        args.append(nc.dram_tensor(f"in_{name}_dram", a.shape, _mybir.dt.from_np(a.dtype), kind="ExternalInput").ap())
    shape = inputs["x"].shape
    args.append(nc.dram_tensor("out_0_dram", shape, _mybir.dt.float32, kind="ExternalOutput").ap())
    build(nc, *args)
    r = _run(nc, [arrays], core_ids=[0])
    return r.results[0]["out_0_dram"]
```
